# Optimizing a Trainium2 kernel written in Bass

```python
import jax, jax.numpy as jnp
from jax import lax
import numpy as np

D_MODEL = 1024
BATCH = 1
SEQ = 256
DEPTH = 4

N_MIXERS = 3
GRID_W = 64
FFN_HIDDEN = -(-8 * D_MODEL // (3 * 256)) * 256
RMS_EPS = 1e-6
LRU_WIDTH = D_MODEL
LRU_HEADS = 8
LRU_BLOCK = LRU_WIDTH // LRU_HEADS
LRU_CONV_W = 4
LRU_C = 8.0
NA_HEADS = 16
NA_HEAD_DIM = D_MODEL // NA_HEADS
NA_WIN_ROWS = 8
NA_WIN_COLS = 16
NEG_INF = -1e30
SC_CONV_W = 3

kernel_name = 'hybrid_lru_natten_shortconv_encoder'

def rms_norm(x, g):
    x32 = x.astype(jnp.float32)
    y = x32 * lax.rsqrt(jnp.mean(x32 * x32, axis=-1, keepdims=True) + RMS_EPS)
    return y.astype(x.dtype) * g

def modulate(h, shift, scale):
    return h * (1 + scale[:, None, :]) + shift[:, None, :]

def depthwise_conv(x, w, pad_left):
    k, ch = w.shape
    return lax.conv_general_dilated(
        x, w[:, None, :], window_strides=(1,),
        padding=[(pad_left, k - 1 - pad_left)],
        dimension_numbers=('NWC', 'WIO', 'NWC'),
        feature_group_count=ch)

def _linear_combine(left, right):
    a_l, b_l = left
    a_r, b_r = right
    return a_l * a_r, a_r * b_l + b_r

def rglru_block(h, w_in, conv_w, conv_b, gate_w, gate_b, lam, w_out):
    bsz, t, _ = h.shape
    y_br, x_br = jnp.split(h @ w_in, 2, axis=-1)
    xc = depthwise_conv(x_br, conv_w, LRU_CONV_W // 2) + conv_b
    xh = xc.reshape(bsz, t, LRU_HEADS, LRU_BLOCK)
    gates = jnp.einsum('btnk,dgnkj->dgbtnj', xh, gate_w).reshape(2, 2, bsz, t, LRU_WIDTH)
    gates = jax.nn.sigmoid((gates + gate_b[:, :, None, None, :]).astype(jnp.float32))
    r, i = gates[:, 0], gates[:, 1]
    log_a = -LRU_C * r * jax.nn.softplus(-lam.astype(jnp.float32))[:, None, None, :]
    a = jnp.exp(log_a)
    b = jnp.sqrt(-jnp.expm1(2.0 * log_a)) * i * xc.astype(jnp.float32)[None]
    _, h_fwd = lax.associative_scan(_linear_combine, (a[0], b[0]), axis=1)
    _, h_bwd = lax.associative_scan(_linear_combine, (a[1], b[1]), axis=1, reverse=True)
    rec = (h_fwd + h_bwd).astype(h.dtype)
    return (rec * jax.nn.gelu(y_br)) @ w_out

def neighbourhood_attention(h, w_qkv, rpb, w_o):
    bsz, t, d = h.shape
    rows = t // GRID_W
    kh = min(NA_WIN_ROWS, rows)
    qkv = (h @ w_qkv).reshape(bsz, rows, GRID_W, 3, NA_HEADS, NA_HEAD_DIM)
    q, k, v = qkv[:, :, :, 0], qkv[:, :, :, 1], qkv[:, :, :, 2]
    row = jnp.arange(rows)
    key_rows = jnp.clip(row - kh // 2, 0, rows - kh)[:, None] + jnp.arange(kh)[None, :]
    k_band = k[:, key_rows].reshape(bsz, rows, kh * GRID_W, NA_HEADS, NA_HEAD_DIM)
    v_band = v[:, key_rows].reshape(bsz, rows, kh * GRID_W, NA_HEADS, NA_HEAD_DIM)
    col = jnp.arange(GRID_W)
    col_start = jnp.clip(col - NA_WIN_COLS // 2, 0, GRID_W - NA_WIN_COLS)
    col_in = (col[None, :] >= col_start[:, None]) & (col[None, :] < col_start[:, None] + NA_WIN_COLS)
    dy = key_rows - row[:, None] + (NA_WIN_ROWS - 1)
    dx = jnp.clip(col[None, :] - col[:, None], -(NA_WIN_COLS - 1), NA_WIN_COLS - 1) + (NA_WIN_COLS - 1)
    bias = rpb[:, dy[:, None, :, None], dx[None, :, None, :]].astype(jnp.float32)
    bias = jnp.where(col_in[None, None, :, None, :], bias, NEG_INF)
    bias = bias.reshape(NA_HEADS, rows, GRID_W, kh * GRID_W)
    scores = jnp.einsum('brqhd,brkhd->bhrqk', q, k_band).astype(jnp.float32) * (NA_HEAD_DIM ** -0.5) + bias[None]
    p = jax.nn.softmax(scores, axis=-1).astype(v.dtype)
    o = jnp.einsum('bhrqk,brkhd->brqhd', p, v_band).reshape(bsz, t, d)
    return o @ w_o

def short_conv_mixer(h, w_in, conv_w, w_out):
    b_gate, c_gate, hx = jnp.split(h @ w_in, 3, axis=-1)
    y = b_gate * depthwise_conv(c_gate * hx, conv_w, SC_CONV_W // 2)
    return y @ w_out

def swiglu(h, w_gu, w_down):
    g, u = jnp.split(h @ w_gu, 2, axis=-1)
    return (jax.nn.silu(g) * u) @ w_down

def setup_inputs(seed: int = 0) -> dict:
    key = jax.random.key(seed)
    ks = jax.random.split(key, 20)
    n_a = (DEPTH + 2) // 3
    n_b = (DEPTH + 1) // 3
    n_c = DEPTH // 3
    f32 = jnp.float32

    def nrm(k, shape, s):
        return jax.random.normal(k, shape, f32) * s

    u = jax.random.uniform(ks[12], (n_a, 2, LRU_WIDTH), f32, 0.9, 0.999)
    p = u ** (1.0 / LRU_C)
    lru_lambda = jnp.log(p) - jnp.log1p(-p)
    return {
        'x': nrm(ks[0], (BATCH, SEQ, D_MODEL), 1.0),
        'c': nrm(ks[1], (BATCH, D_MODEL), 1.0),
        'ada_w': nrm(ks[2], (DEPTH, D_MODEL, 6 * D_MODEL), D_MODEL ** -0.5),
        'ada_b': nrm(ks[3], (DEPTH, 6 * D_MODEL), 0.01),
        'norm_g': 1.0 + nrm(ks[4], (DEPTH, 4, D_MODEL), 0.05),
        'ffn_w_gu': nrm(ks[5], (DEPTH, D_MODEL, 2 * FFN_HIDDEN), D_MODEL ** -0.5),
        'ffn_w_down': nrm(ks[6], (DEPTH, FFN_HIDDEN, D_MODEL), FFN_HIDDEN ** -0.5),
        'lru_w_in': nrm(ks[7], (n_a, D_MODEL, 2 * LRU_WIDTH), D_MODEL ** -0.5),
        'lru_conv_w': nrm(ks[8], (n_a, LRU_CONV_W, LRU_WIDTH), LRU_CONV_W ** -0.5),
        'lru_conv_b': nrm(ks[9], (n_a, LRU_WIDTH), 0.01),
        'lru_gate_w': nrm(ks[10], (n_a, 2, 2, LRU_HEADS, LRU_BLOCK, LRU_BLOCK), LRU_BLOCK ** -0.5),
        'lru_gate_b': nrm(ks[11], (n_a, 2, 2, LRU_WIDTH), 0.01),
        'lru_lambda': lru_lambda,
        'lru_w_out': nrm(ks[13], (n_a, LRU_WIDTH, D_MODEL), LRU_WIDTH ** -0.5),
        'na_w_qkv': nrm(ks[14], (n_b, D_MODEL, 3 * D_MODEL), D_MODEL ** -0.5),
        'na_rpb': nrm(ks[15], (n_b, NA_HEADS, 2 * NA_WIN_ROWS - 1, 2 * NA_WIN_COLS - 1), 0.02),
        'na_w_o': nrm(ks[16], (n_b, D_MODEL, D_MODEL), D_MODEL ** -0.5),
        'sc_w_in': nrm(ks[17], (n_c, D_MODEL, 3 * D_MODEL), D_MODEL ** -0.5),
        'sc_conv_w': nrm(ks[18], (n_c, SC_CONV_W, D_MODEL), SC_CONV_W ** -0.5),
        'sc_w_out': nrm(ks[19], (n_c, D_MODEL, D_MODEL), D_MODEL ** -0.5),
    }

def reference(x, c, ada_w, ada_b, norm_g, ffn_w_gu, ffn_w_down,
              lru_w_in, lru_conv_w, lru_conv_b, lru_gate_w, lru_gate_b, lru_lambda, lru_w_out,
              na_w_qkv, na_rpb, na_w_o, sc_w_in, sc_conv_w, sc_w_out):
    c_act = jax.nn.silu(c)
    for i in range(DEPTH):
        mod = c_act @ ada_w[i] + ada_b[i]
        sh_m, sc_m, g_m, sh_f, sc_f, g_f = jnp.split(mod, 6, axis=-1)
        h = modulate(rms_norm(x, norm_g[i, 0]), sh_m, sc_m)
        kind, j = i % N_MIXERS, i // N_MIXERS
        if kind == 0:
            m = rglru_block(h, lru_w_in[j], lru_conv_w[j], lru_conv_b[j], lru_gate_w[j],
                            lru_gate_b[j], lru_lambda[j], lru_w_out[j])
        elif kind == 1:
            m = neighbourhood_attention(h, na_w_qkv[j], na_rpb[j], na_w_o[j])
        else:
            m = short_conv_mixer(h, sc_w_in[j], sc_conv_w[j], sc_w_out[j])
        x = x + g_m[:, None, :] * rms_norm(m, norm_g[i, 1])
        h = modulate(rms_norm(x, norm_g[i, 2]), sh_f, sc_f)
        f = swiglu(h, ffn_w_gu[i], ffn_w_down[i])
        x = x + g_f[:, None, :] * rms_norm(f, norm_g[i, 3])
    return x


_drawn_inputs = setup_inputs


def setup_inputs(seed=0):
    import zlib

    import numpy as np

    out = dict(_drawn_inputs(seed))
    spreads = {}
    factors = {'lru_conv_b': 4.549, 'lru_gate_b': 23.604, 'na_rpb': 8.0}
    for name, (base, spread) in spreads.items():
        noise = np.random.default_rng([zlib.crc32(name.encode()), seed]).standard_normal(out[name].shape)
        drawn = base * np.exp(spread * noise) if base else spread * noise
        out[name] = __import__('jax').numpy.asarray(drawn.astype(out[name].dtype))
    for name, factor in factors.items():
        out[name] = (out[name] * factor).astype(out[name].dtype)
    return out
```

```python
import concourse.bass as bass
import numpy as np
from concourse import mybir
from concourse.alu_op_type import AluOpType as ALU
from contextlib import ExitStack

P = 128
D_MODEL, SEQ, DEPTH = 1024, 256, 4
KC = D_MODEL // P
TT = SEQ // P
HALF = 512
FFN_HIDDEN = 2816
FC = FFN_HIDDEN // P
EPS = 1e-6
LRU_C = 8.0
HEADS, HEAD_DIM = 16, 64
GRID_W, ROWS = 64, 4
RPB_ROWS, RPB_COLS = 15, 31
BAND = 6
NEG = -1e30

BLOCK = 2048
SLOTS = 3
LRU, ATTENTION, SHORT_CONV = 0, 1, 2
KINDS = [i % 3 for i in range(DEPTH)]
MIX_UP = {LRU: 8, ATTENTION: 8, SHORT_CONV: 12}
MIX_MID = {LRU: 2, ATTENTION: 4, SHORT_CONV: 0}
OUT_BLOCKS = D_MODEL // (2 * P)
FFN_DOWN = FC // 2

ADA_COLS = 384
ADA_BLOCKS = DEPTH * 6 * D_MODEL // ADA_COLS
ADA_FIRST = 6


def _layout():
    layers, b, q = [], 0, 0
    for i, kind in enumerate(KINDS):
        mix = dict(b=b, q=q, act=(KC + FC) * i, up=MIX_UP[kind], mid=MIX_MID[kind])
        mix["out"] = b + mix["up"] + mix["mid"]
        b, q = mix["out"] + OUT_BLOCKS, q + mix["up"]
        ffn = dict(b=b, act=(KC + FC) * i + KC, up=FC)
        ffn["out"] = b + FC
        b = ffn["out"] + FFN_DOWN
        mix["end"], ffn["end"] = ffn["b"], b
        layers.append((kind, mix, ffn))
    return layers, b


LAYERS, BLOCKS = _layout()
ROUNDS = BLOCKS // SLOTS


def ada_after(b):
    r, s = divmod(b, SLOTS)
    if r <= 4:
        return {0: None, 1: ADA_FIRST + 2 * r, 2: ADA_FIRST + 1 + 2 * r}[s]
    return r + 11 if s == 2 and r + 11 < ADA_BLOCKS else None


COL_C = 0
COL_ADA_B = COL_C + KC
COL_NORM = COL_ADA_B + DEPTH * 6 * KC
COL_LRU = COL_NORM + DEPTH * 2 * KC
LRU_COLS = (4 + 1 + 4 + 2) * KC
N_LRU = KINDS.count(LRU)
COL_SC = COL_LRU + N_LRU * LRU_COLS
COLS = COL_SC + 3 * KC


def encoder(nc, stream, ada, cols, x_in, norm_g, ada_b, rpb, out):
    f32, f32r, bf16 = mybir.dt.float32, mybir.dt.float32r, mybir.dt.bfloat16
    ACT = mybir.ActivationFunctionType
    ctx = ExitStack()
    with ctx:
        def sb(name, shape, dtype=f32):
            return ctx.enter_context(nc.sbuf_tensor(name, shape, dtype))

        def sem(name):
            return ctx.enter_context(nc.semaphore(name))

        base = -(-nc.sbuf_base // 32) * 32
        h_hi = sb("h_hi", [P, KC, SEQ], f32r)
        h_lo = sb("h_lo", [P, KC, SEQ], f32r)
        act_hi = sb("act_hi", [P, FC, SEQ], f32r)
        act_lo = sb("act_lo", [P, FC, SEQ], f32r)
        chunk = SEQ * 4
        at_h_lo, at_act_hi = base + KC * chunk, base + 2 * KC * chunk
        at_act_lo = at_act_hi + FC * chunk

        def over(name, shape, offset):
            return nc.alloc_sbuf_tensor_at(name, shape, f32, offset=offset)

        lru_r = [over("lru_r0", [P, KC, SEQ], at_act_hi + KC * chunk),
                 over("lru_r1", [P, KC, SEQ], at_act_lo + KC * chunk)]
        lru_a = [over("lru_a0", [P, KC, SEQ], at_act_hi), over("lru_a1", [P, KC, SEQ], at_act_lo)]
        lru_i = [over("lru_i0", [P, KC, SEQ], base), over("lru_i1", [P, KC, SEQ], at_h_lo)]
        bands = [over("band0", [P, HEADS // 2, BAND, GRID_W], at_act_hi + KC * chunk),
                 over("band1", [P, HEADS // 2, BAND, GRID_W], at_act_lo + KC * chunk)]
        probs = over("probs", [P, 4, TT, SEQ], base)
        probs_t = over("probs_t", [P, 4, TT, SEQ], at_h_lo)
        ada_extra = [over(f"ada_extra{i}", [P, KC, ADA_COLS], at_act_hi + i * KC * ADA_COLS * 4)
                     for i in range(3)]

        raw = sb("raw", [P, SLOTS, BLOCK])
        w_hi = sb("w_hi", [P, SLOTS, BLOCK], f32r)
        w_lo = sb("w_lo", [P, SLOTS, BLOCK], f32r)
        ada_raw = sb("ada_raw", [P, KC, ADA_COLS])
        ada_acc = sb("ada_acc", [P, ADA_COLS])
        ada_sum = sb("ada_sum", [P, ADA_COLS])
        x = sb("x", [P, TT, D_MODEL])
        buf_a = sb("buf_a", [P, KC * SEQ])
        buf_b = sb("buf_b", [P, KC * SEQ])
        buf_c = sb("buf_c", [P, KC * SEQ])
        tok = buf_a[:, :].rearrange("p (t d) -> p t d", t=TT)
        feat_a = buf_a[:, :].rearrange("p (k s) -> p k s", k=KC)
        feat_b = buf_b[:, :].rearrange("p (k s) -> p k s", k=KC)
        feat_c = buf_c[:, :].rearrange("p (k s) -> p k s", k=KC)
        values = buf_c[:, :].rearrange("p (t d) -> p t d", t=TT)
        gate_row = sb("gate_row", [P, D_MODEL])
        bias_row = sb("bias_row", [P, D_MODEL])
        norm_row = sb("norm_row", [P, D_MODEL])
        side = sb("side", [P, SLOTS, SEQ])
        prod = sb("prod", [P, SLOTS, SEQ])
        junk = sb("junk", [P, 4, HALF], bf16)
        col = sb("col", [P, COLS])
        c_act = sb("c_act", [P, KC])
        mod_row = sb("mod_row", [2 * KC, P])
        mod_col = sb("mod_col", [P, 2 * KC])
        scale_col = sb("scale_col", [P, KC])
        lam_n = N_LRU * 2 * KC
        soft = sb("soft", [P, 6, lam_n])
        stat = sb("stat", [P, 24])
        sq_m, sq_x, tmp, rs_m, rs_x = (stat[:, a:a + n] for a, n in
                                       ((0, 4), (4, 4), (8, 2), (10, 2), (12, 2)))
        minus_half = stat[:, 14:15]
        smax = sb("smax", [P, 4, TT])
        sneg = sb("sneg", [P, 4, TT])
        ssum = sb("ssum", [P, 4, TT])
        sinv = sb("sinv", [P, 4, TT])
        ident = sb("ident", [P, P])

        up = ctx.enter_context(nc.psum_tensor("up", [P, 4, HALF], f32))
        down = ctx.enter_context(nc.psum_tensor("down", [P, TT, 2, HALF], f32))
        mod_dram = nc.dram_tensor("mod_scratch", [ADA_BLOCKS, ADA_COLS], f32)
        mod_rows = mod_dram.ap().rearrange("a (o c) -> a o c", o=1)

        raw_in = [sem(f"raw_in{s}") for s in range(SLOTS)]
        hi_ready, lo_ready, block_used = sem("hi_ready"), sem("lo_ready"), sem("block_used")
        cols_in, x_loaded = sem("cols_in"), sem("x_loaded")
        ada_in, ada_extra_in = sem("ada_in"), [sem(f"ada_extra_in{i}") for i in range(3)]
        acc_step, acc_ready, acc_free = sem("acc_step"), sem("acc_ready"), sem("acc_free")
        mod_out, mod_row_in, rows_in = sem("mod_out"), sem("mod_row_in"), sem("rows_in")
        mod_t_done, mod_col_step, mod_col_ready = sem("mod_t_done"), sem("mod_col_step"), sem("mod_col_ready")
        sum_turn = sem("sum_turn")
        gate_row_ready = sem("gate_row_ready")
        ident_ready, consts_ready, c_ready = sem("ident_ready"), sem("consts_ready"), sem("c_ready")
        soft_exp, soft_step = sem("soft_exp"), sem("soft_step")
        sq_m_ready, sq_x_ready = sem("sq_m_ready"), sem("sq_x_ready")
        rs_step, rs_m_ready, rs_x_ready = sem("rs_step"), sem("rs_m_ready"), sem("rs_x_ready")
        delta_ready, x_ready, xn_ready = sem("delta_ready"), sem("x_ready"), sem("xn_ready")
        xt_done, h_ready, h_hi_ready, h_lo_ready = sem("xt_done"), sem("h_ready"), sem("h_hi_ready"), sem("h_lo_ready")
        up_free, down_done = sem("up_free"), sem("down_done")
        side_ready = sem("side_ready")
        prod_ready, act_hi_ready, act_lo_ready = sem("prod_ready"), sem("act_hi_ready"), sem("act_lo_ready")
        conv_ready, conv_step, xc_hi_ready, xc_lo_ready = sem("conv_ready"), sem("conv_step"), sem("xc_hi_ready"), sem("xc_lo_ready")
        gates_done, gates_free, y_ready, ix_ready = sem("gates_done"), sem("gates_free"), sem("y_ready"), sem("ix_ready")
        decay_ready, w_ready, root_ready, vector_step = sem("decay_ready"), sem("w_ready"), sem("root_ready"), sem("vector_step")
        q_ready, v_done, v_ready, band_in, band_ready = sem("q_ready"), sem("v_done"), sem("v_ready"), sem("band_in"), sem("band_ready")
        scores_done, score_ready, neg_ready, exp_ready = sem("scores_done"), sem("score_ready"), sem("neg_ready"), sem("exp_ready")
        inv_ready, probs_ready, pt_done, pt_ready, pv_done = sem("inv_ready"), sem("probs_ready"), sem("pt_done"), sem("pt_ready"), sem("pv_done")
        stored = sem("stored")

        block = ctx.enter_context(nc.Block())

        def wait(eng, s, value):
            if not isinstance(value, int) or value > 0:
                eng.wait_ge(s, value)

        def each_block(eng, first, n, body):
            b, end = first, first + n
            while b < end and (b % SLOTS or b < SLOTS):
                body(b, b % SLOTS, b // SLOTS)
                b += 1
            rounds = (end - b) // SLOTS
            if rounds > 1:
                with eng.Fori(b // SLOTS, b // SLOTS + rounds) as r:
                    for s in range(SLOTS):
                        body(r * SLOTS + s, s, r)
                b += rounds * SLOTS
            while b < end:
                body(b, b % SLOTS, b // SLOTS)
                b += 1

        def straight(eng, first, n, body):
            for b in range(first, first + n):
                body(b, b % SLOTS, b // SLOTS)

        def norm_bank(v):
            s = first_slot(v)
            banks = [up[:, 3, :], up[:, (s + 1) % SLOTS, :], up[:, (s + 2) % SLOTS, :], down[:, 0, 0, :]]
            return [banks[k // 2][:, (k % 2) * SEQ:(k % 2 + 1) * SEQ] for k in range(KC)]

        def first_slot(v):
            return LAYERS[v // 2][1 + v % 2]["b"] % SLOTS

        @block.sync
        def _(sp):
            def load(m, s):
                wait(sp, lo_ready, m - SLOTS + 1)
                sp.dma_start(raw[:, s, :], stream[m]).then_inc(raw_in[s], 16)

            def load_ada(a):
                wait(sp, acc_ready, a)
                sp.dma_start(ada_raw[:, :, :], ada[a]).then_inc(ada_in, 16)

            sp.dma_start(col[:, :], cols).then_inc(cols_in, 16)
            sp.dma_start(ada_raw[:, :, :], ada[0]).then_inc(ada_in, 16)
            for i in range(3):
                sp.dma_start(ada_extra[i][:, :, :], ada[1 + i]).then_inc(ada_extra_in[i], 16)
            sp.wait_ge(acc_ready, 1)
            sp.dma_start(ada_raw[:, :, :], ada[4]).then_inc(ada_in, 16)
            sp.wait_ge(acc_ready, 2)
            sp.dma_start(ada_extra[0][:, :, :], ada[5]).then_inc(ada_extra_in[0], 16)
            for t in range(TT):
                sp.dma_start(x[:, t, :], x_in[t * P:(t + 1) * P, :]).then_inc(x_loaded, 16)
            for s in range(SLOTS):
                load(s, s)
            sp.wait_ge(acc_ready, 5)
            sp.dma_start(ada_raw[:, :, :], ada[6]).then_inc(ada_in, 16)
            for m in range(SLOTS, 7 * SLOTS):
                load(m, m % SLOTS)
                if m >= 2 * SLOTS and ada_after(m - 2 * SLOTS) is not None:
                    load_ada(ada_after(m - 2 * SLOTS) + 1)
            with sp.Fori(7, ADA_BLOCKS - 10) as r:
                for s in range(SLOTS):
                    load(r * SLOTS + s, s)
                load_ada(r + 10)
            with sp.Fori(ADA_BLOCKS - 10, ROUNDS) as r:
                for s in range(SLOTS):
                    load(r * SLOTS + s, s)
            for t in range(TT):
                sp.wait_ge(x_ready, 4 * (2 * DEPTH - 1) + 2 * (t + 1))
                sp.dma_start(out[t * P:(t + 1) * P, :], x[:, t, :]).then_inc(stored, 16)
            sp.wait_ge(stored, 16 * TT)

        @block.tensor
        def _(pe):
            def three(dst, w, act_of, k, cols_w, cols_a, weights_stationary, start, stop, check=False):
                hi_a, lo_a = act_of
                terms = ((w_hi, hi_a), (w_hi, lo_a), (w_lo, hi_a))
                for n, (wt, at) in enumerate(terms):
                    wv, av = wt[:, w, cols_w], at[:, k, cols_a]
                    lhs, rhs = (wv, av) if weights_stationary else (av, wv)
                    last = nc.tensor.matmul(dst, lhs, rhs, start=start and n == 0, stop=stop and n == 2,
                                            skip_group_check=check)
                return last

            def transposes(v):
                s0 = first_slot(v)
                pe.wait_ge(mod_row_in, 16 * (v + 1))
                nc.tensor.transpose(up[:, s0, 0:2 * KC], mod_row[:, :], ident[0:2 * KC, 0:2 * KC])\
                    .then_inc(mod_t_done, 1)
                dst = norm_bank(v)
                for t in range(TT):
                    pe.wait_ge(xn_ready, 2 * v + t + 1)
                    for k in range(KC):
                        last = nc.tensor.transpose(dst[k][:, t * P:(t + 1) * P],
                                                   tok[:, t, k * P:(k + 1) * P], ident[:, :])
                        if t == TT - 1:
                            last.then_inc(xt_done, 1)

            def up_phase(v, b0, n, free, q0):
                def body(b, s, r):
                    pe.wait_ge(lo_ready, b + 1)
                    first = isinstance(b, int) and b == b0
                    if isinstance(b, int):
                        wait(pe, free, q0 + max(b - b0 - 2, 0))
                    else:
                        pe.wait_ge(free, b + (q0 - b0 - 2))
                    for k in range(KC):
                        if first:
                            pe.wait_ge(h_lo_ready, KC * v + k + 1)
                        for o in range(2):
                            c0 = (2 * k + o) * P
                            last = three(up[:, s, o * SEQ:(o + 1) * SEQ], s, (h_hi, h_lo), k,
                                         slice(c0, c0 + P), slice(0, SEQ), True,
                                         start=k == 0 and o == 0, stop=k == KC - 1, check=True)
                    last.then_inc(block_used, 1)
                body(b0, b0 % SLOTS, b0 // SLOTS)
                each_block(pe, b0 + 1, n - 1, body)

            def down_phase(acts, b0, n, act_base, done, chunks_ready):
                for j in range(n):
                    b = b0 + j
                    s = b % SLOTS
                    pe.wait_ge(lo_ready, b + 1)
                    if chunks_ready is not None:
                        pe.wait_ge(chunks_ready, act_base + 2 * j + 2)
                    for t in range(TT):
                        for h in range(2):
                            for kk in range(2):
                                c0 = kk * D_MODEL + h * HALF
                                last = three(down[:, t, h, :], s, acts, 2 * j + kk,
                                             slice(c0, c0 + HALF), slice(t * P, (t + 1) * P), False,
                                             start=j == 0 and kk == 0, stop=j == n - 1 and kk == 1)
                            if j == n - 1 and (t, h) != (TT - 1, 1):
                                last.then_inc(done, 1)
                    last.then_inc(block_used, 1)

            def gate_phase(mix, li):
                for d in range(2):
                    b = mix["b"] + mix["up"] + d
                    s = b % SLOTS
                    pe.wait_ge(lo_ready, b + 1)
                    for n in range(KC):
                        pair = KC * d + n
                        if d == 0:
                            pe.wait_ge(xc_lo_ready, KC * li + n + 1)
                        wait(pe, gates_free, 2 * KC * li + pair - 3 if pair > 3 else 0)
                        for g in range(2):
                            c0 = (2 * n + g) * P
                            last = three(down[:, (pair % 4) // 2, pair % 2, g * SEQ:(g + 1) * SEQ], s,
                                         (act_hi, act_lo), n, slice(c0, c0 + P), slice(0, SEQ), True,
                                         start=g == 0, stop=True, check=True)
                        last.then_inc(gates_done if n < KC - 1 else block_used, 1)

            def attention(mix):
                def scores(h):
                    p0, n = HEAD_DIM * (h % 2), h // 2
                    if h == 0:
                        pe.wait_ge(up_free, mix["q"] + mix["up"])
                    wait(pe, score_ready, TT * (h - 1))
                    for t in range(TT):
                        last = nc.tensor.matmul(up[:, h % 2, t * SEQ:(t + 1) * SEQ],
                                                feat_a[p0:p0 + HEAD_DIM, n, t * P:(t + 1) * P],
                                                feat_b[p0:p0 + HEAD_DIM, n, :],
                                                start=True, stop=True)
                    last.then_inc(scores_done, 1)

                def transpose_probs(h):
                    pe.wait_ge(probs_ready, TT * (h + 1))
                    wait(pe, pt_ready, h - 1)
                    for t in range(TT):
                        for kt in range(TT):
                            last = nc.tensor.transpose(
                                up[:, 2 + h % 2, kt * SEQ + t * P:kt * SEQ + (t + 1) * P],
                                probs[:, h % 4, t, kt * P:(kt + 1) * P], ident[:, :])
                    last.then_inc(pt_done, 1)

                def mix_values(h):
                    p0, n = HEAD_DIM * (h % 2), h // 2
                    pe.wait_ge(pt_ready, h + 1)
                    if n >= 4 and h % 2 == 0:
                        pe.wait_ge(act_lo_ready, mix["act"] + n - 3)
                    for kt in range(TT):
                        last = nc.tensor.matmul(down[p0:p0 + HEAD_DIM, (n % 4) // 2, n % 2, 0:SEQ],
                                                values[:, kt, h * HEAD_DIM:(h + 1) * HEAD_DIM],
                                                probs_t[:, h % 4, kt, :],
                                                start=kt == 0, stop=kt == TT - 1)
                    last.then_inc(pv_done, 1)

                pe.wait_ge(v_ready, 4)
                for h in range(HEADS + 2):
                    if h < HEADS:
                        scores(h)
                    if 1 <= h <= HEADS:
                        transpose_probs(h - 1)
                    if h >= 2:
                        mix_values(h - 2)
                pe.wait_ge(act_lo_ready, mix["act"] + KC)

            pe.wait_ge(ident_ready, 2)
            li = 0
            for i, (kind, mix, ffn) in enumerate(LAYERS):
                transposes(2 * i)
                up_phase(2 * i, mix["b"], mix["up"], up_free, mix["q"])
                if kind == LRU:
                    gate_phase(mix, li)
                    li += 1
                elif kind == ATTENTION:
                    down_phase((h_hi, h_lo), mix["b"] + mix["up"], mix["mid"], 0, v_done, None)
                    attention(mix)
                down_phase((act_hi, act_lo), mix["out"], OUT_BLOCKS, mix["act"], down_done, act_lo_ready)
                transposes(2 * i + 1)
                up_phase(2 * i + 1, ffn["b"], ffn["up"], prod_ready, ffn["prod"])
                down_phase((act_hi, act_lo), ffn["out"], FFN_DOWN, ffn["act"], down_done, act_lo_ready)

        @block.scalar
        def _(act):
            def round_block(b, s, r):
                if isinstance(b, int) and b >= BLOCKS:
                    return
                act.wait_ge(raw_in[s], r * 16 + 16)
                wait(act, block_used, b - SLOTS + 1)
                nc.scalar.activation(w_hi[:, s, :], raw[:, s, :], ACT.Copy).then_inc(hi_ready, 1)

            def squares_m(u):
                for n in range(4):
                    if n < 3:
                        act.wait_ge(down_done, 3 * u + n + 1)
                    else:
                        act.wait_ge(block_used, LAYERS[u // 2][1 + u % 2]["end"])
                    nc.scalar.activation(junk[:, n, :], down[:, n // 2, n % 2, :], ACT.Square,
                                         accum_out=sq_m[:, n:n + 1]).then_inc(sq_m_ready, 1)

            def pre_norm(v):
                for n in range(4):
                    if v == 0:
                        act.wait_ge(x_loaded, 16 * TT)
                    else:
                        act.wait_ge(x_ready, 4 * (v - 1) + n + 1)
                    nc.scalar.activation(junk[:, n, :], x[:, n // 2, (n % 2) * HALF:(n % 2 + 1) * HALF],
                                         ACT.Square, accum_out=sq_x[:, n:n + 1]).then_inc(sq_x_ready, 1)
                src = norm_bank(v)
                act.wait_ge(mod_col_ready, v + 1)
                for k in range(KC):
                    act.wait_ge(xt_done, KC * v + (k | 1) + 1)
                    nc.scalar.activation(feat_b[:, k, :], src[k], ACT.Identity,
                                         scale=scale_col[:, k:k + 1], bias=mod_col[:, k:k + 1])\
                        .then_inc(h_ready, 1)

            def ffn_up(ffn):
                def body(b, s, r):
                    j = b - ffn["b"]
                    act.wait_ge(block_used, b + 1)
                    nc.scalar.activation(side[:, s, :], up[:, s, 0:SEQ], ACT.Silu).then_inc(side_ready, 1)
                    round_block(b + SLOTS, s, r + 1)
                    act.wait_ge(prod_ready, j + ffn["prod"] + 1)
                    nc.scalar.activation(act_hi[:, j, :], prod[:, s, :], ACT.Copy).then_inc(act_hi_ready, 1)
                each_block(act, ffn["b"], ffn["up"], body)

            def down_rounds(first, n):
                n = min(n, BLOCKS - SLOTS - first)
                each_block(act, first, n, lambda b, s, r: round_block(b + SLOTS, s, r + 1))

            def lru(mix, li):
                c0 = COL_LRU + li * LRU_COLS

                def body(b, s, r):
                    n = b - mix["b"]
                    act.wait_ge(block_used, b + 1)
                    nc.scalar.activation(feat_c[:, n, :], up[:, s, 0:SEQ], ACT.Gelu_apprx_tanh)
                    nc.scalar.activation(feat_b[:, n, :], up[:, s, SEQ:2 * SEQ], ACT.Identity,
                                         scale=col[:, c0 + 2 * KC + n:c0 + 2 * KC + n + 1],
                                         bias=col[:, c0 + 4 * KC + n:c0 + 4 * KC + n + 1])\
                        .then_inc(conv_ready, 1)
                    round_block(b + SLOTS, s, r + 1)
                straight(act, mix["b"], mix["up"], body)
                for d in range(2):
                    for n in range(KC):
                        pair = KC * d + n
                        b = mix["b"] + mix["up"] + d
                        if n < KC - 1:
                            act.wait_ge(gates_done, (2 * li + d) * (KC - 1) + n + 1)
                        else:
                            act.wait_ge(block_used, b + 1)
                        for g, dst in ((0, lru_r[d]), (1, lru_i[d])):
                            cb = c0 + (5 + 2 * d + g) * KC + n
                            last = nc.scalar.activation(dst[:, n, :],
                                                        down[:, (pair % 4) // 2, pair % 2, g * SEQ:(g + 1) * SEQ],
                                                        ACT.Sigmoid, bias=col[:, cb:cb + 1])
                        last.then_inc(gates_free, 1)
                    round_block(b + SLOTS, b % SLOTS, b // SLOTS + 1)
                for d in range(2):
                    act.wait_ge(y_ready, 2 * KC * li + KC * (d + 1))
                    act.wait_ge(block_used, mix["out"])
                    squared = (feat_a, feat_b)[d]
                    if d == 1:
                        act.wait_ge(ix_ready, 2 * KC * (li + 1))
                    nc.scalar.activation(squared, lru_r[d][:, :, :], ACT.Exp, scale=-2.0).then_inc(decay_ready, 1)
                    nc.scalar.activation(lru_a[d][:, :, :], lru_r[d][:, :, :], ACT.Exp, scale=-1.0)\
                        .then_inc(decay_ready, 1)
                    act.wait_ge(decay_ready, 6 * li + 3 * d + 2)
                    nc.scalar.activation(lru_r[d][:, :, :], lru_r[d][:, :, :], ACT.Tanh).then_inc(decay_ready, 1)
                for d in range(2):
                    act.wait_ge(w_ready, 2 * li + d + 1)
                    nc.scalar.activation(lru_r[d][:, :, :], lru_r[d][:, :, :], ACT.Sqrt).then_inc(root_ready, 1)
                for n in range(KC):
                    act.wait_ge(prod_ready, mix["prod"] + n + 1)
                    nc.scalar.activation(act_hi[:, n, :], feat_b[:, n, :], ACT.Copy).then_inc(act_hi_ready, 1)

            def by_row(v):
                return v.rearrange("p (r c) -> p r c", c=GRID_W)

            def attention(mix):
                for half in range(2):
                    for rl in range(2):
                        for j in range(BAND):
                            row = half * HEADS // 2 * RPB_ROWS + j + 5 - rl
                            off = row * RPB_COLS + RPB_COLS // 2 - (GRID_W - 1)
                            src = bass.AP(rpb.tensor, off, [[1, GRID_W], [RPB_ROWS * RPB_COLS, HEADS // 2],
                                                            [1, GRID_W]])
                            act.dma_start(bands[half][rl * GRID_W:(rl + 1) * GRID_W, :, j, :], src)\
                                .then_inc(band_in, 16)

                def body(b, s, r):
                    n = b - mix["b"]
                    act.wait_ge(block_used, b + 1)
                    nc.scalar.activation(by_row(feat_a[:, n, :])[:, :, ::-1], by_row(up[:, s, 0:SEQ]), ACT.Copy,
                                         scale=HEAD_DIM ** -0.5).then_inc(q_ready, 1)
                    round_block(b + SLOTS, s, r + 1)
                straight(act, mix["b"], mix["up"], body)
                down_rounds(mix["b"] + mix["up"], mix["mid"])
                for n in range(4):
                    if n < 3:
                        act.wait_ge(v_done, n + 1)
                    else:
                        act.wait_ge(block_used, mix["out"])
                    nc.scalar.activation(values[:, n // 2, (n % 2) * HALF:(n % 2 + 1) * HALF],
                                         down[:, n // 2, n % 2, :], ACT.Copy).then_inc(v_ready, 1)
                for h in range(HEADS + 3):
                    if h < HEADS:
                        act.wait_ge(neg_ready, h + 1)
                        for t in range(TT):
                            nc.scalar.activation(probs[:, h % 4, t, :], probs[:, h % 4, t, :], ACT.Exp,
                                                 bias=sneg[:, h % 4, t:t + 1],
                                                 accum_out=ssum[:, h % 4, t:t + 1]).then_inc(exp_ready, 1)
                    if 1 <= h <= HEADS:
                        act.wait_ge(pt_done, h)
                        wait(act, pv_done, h - 4)
                        nc.scalar.activation(by_row(probs_t[:, (h - 1) % 4, :, :].rearrange("p t s -> p (t s)")),
                                             by_row(up[:, 2 + (h - 1) % 2, :])[:, :, ::-1], ACT.Copy)\
                            .then_inc(pt_ready, 1)
                    if h >= 4 and h % 2 == 0:
                        n = (h - 4) // 2
                        act.wait_ge(pv_done, 2 * n + 2)
                        nc.scalar.activation(act_hi[:, n, :], down[:, (n % 4) // 2, n % 2, 0:SEQ],
                                             ACT.Copy).then_inc(act_hi_ready, 1)

            def short_conv(mix):
                def pair(b, s, r):
                    n = b - mix["b"]
                    act.wait_ge(block_used, b + 1)
                    nc.scalar.activation(side[:, s, :], up[:, s, SEQ:2 * SEQ], ACT.Copy).then_inc(side_ready, 1)
                    round_block(b + SLOTS, s, r + 1)
                    act.wait_ge(up_free, mix["q"] + n + 1)
                    nc.scalar.activation(feat_c[:, n, :], feat_b[:, n, :], ACT.Copy,
                                         scale=col[:, COL_SC + KC + n:COL_SC + KC + n + 1]).then_inc(conv_ready, 1)
                straight(act, mix["b"], KC, pair)

                def gate(b, s, r):
                    j = b - mix["b"] - KC
                    round_block(b + SLOTS, s, r + 1)
                    act.wait_ge(up_free, mix["q"] + KC + j + 1)
                    for n in (2 * j, 2 * j + 1):
                        nc.scalar.activation(act_hi[:, n, :], feat_a[:, n, :], ACT.Copy).then_inc(act_hi_ready, 1)
                straight(act, mix["b"] + KC, mix["up"] - KC, gate)

            act.wait_ge(cols_in, 16)
            nc.scalar.activation(c_act[:, :], col[:, COL_C:COL_C + KC], ACT.Silu).then_inc(c_ready, 1)
            act.wait_ge(soft_step, 1)
            nc.scalar.activation(soft[:, 1, :], soft[:, 0, :], ACT.Exp, scale=-1.0).then_inc(soft_exp, 1)
            for b in range(SLOTS):
                round_block(b, b, 0)
            pre_norm(0)
            li = 0
            for i, (kind, mix, ffn) in enumerate(LAYERS):
                if kind == LRU:
                    lru(mix, li)
                    li += 1
                elif kind == ATTENTION:
                    attention(mix)
                else:
                    short_conv(mix)
                down_rounds(mix["out"], OUT_BLOCKS - 1)
                squares_m(2 * i)
                pre_norm(2 * i + 1)
                down_rounds(mix["end"] - 1, 1)
                ffn_up(ffn)
                down_rounds(ffn["out"], FFN_DOWN - 1)
                squares_m(2 * i + 1)
                if i < DEPTH - 1:
                    pre_norm(2 * i + 2)
                    down_rounds(ffn["end"] - 1, 1)

        @block.vector
        def _(dve):
            steps = [0, 0]

            def link(last, which=0):
                s = (soft_step, vector_step)[which]
                steps[which] += 1
                last.then_inc(s, 1)
                dve.wait_ge(s, steps[which])

            def lo_block(b, s):
                if isinstance(b, int) and b >= BLOCKS:
                    return
                dve.wait_ge(hi_ready, b + 1)
                nc.vector.tensor_tensor(w_lo[:, s, :], raw[:, s, :], w_hi[:, s, :].bitcast(f32),
                                        ALU.subtract).then_inc(lo_ready, 1)

            def ada_block(a, src, arrived, count):
                dve.wait_ge(arrived, count)
                wait(dve, acc_free, a)
                nc.vector.tensor_scalar(ada_acc[:, :], src[:, 0, :], c_act[:, 0:1], None, ALU.mult)\
                    .then_inc(acc_step, 1)
                for k in range(1, KC):
                    dve.wait_ge(acc_step, a * (KC - 1) + k)
                    last = nc.vector.scalar_tensor_tensor(ada_acc[:, :], src[:, k, :], c_act[:, k:k + 1],
                                                          ada_acc[:, :], ALU.mult, ALU.add)
                    last.then_inc(acc_step if k < KC - 1 else acc_ready, 1)

            def prepare(b, s, r):
                lo_block(b + SLOTS, s)
                if isinstance(b, int):
                    a = ada_after(b)
                    if a is not None:
                        ada_block(a, ada_raw, ada_in, 16 * (a - 3))
                elif s == SLOTS - 1 and ada_in_loop[0]:
                    ada_block(r + 11, ada_raw, ada_in, r * 16 + 16 * 8)

            ada_in_loop = [True]

            def post_norm(u):
                dve.wait_ge(gate_row_ready, u + 1)
                for n in range(4):
                    t, cs = n // 2, slice((n % 2) * HALF, (n % 2 + 1) * HALF)
                    dve.wait_ge(rs_m_ready, 2 * u + t + 1)
                    nc.vector.scalar_tensor_tensor(tok[:, t, cs], down[:, t, n % 2, :], rs_m[:, t:t + 1],
                                                   gate_row[:, cs], ALU.mult, ALU.mult).then_inc(delta_ready, 1)
                    dve.wait_ge(delta_ready, 4 * u + n + 1)
                    nc.vector.tensor_tensor(x[:, t, cs], x[:, t, cs], tok[:, t, cs], ALU.add)\
                        .then_inc(x_ready, 1)

            def modulation(v):
                i, part = divmod(v, 2)
                dve.wait_ge(mod_t_done, v + 1)
                cb = COL_ADA_B + (6 * i + 3 * part) * KC
                nc.vector.tensor_tensor(mod_col[:, :], up[:, first_slot(v), 0:2 * KC],
                                        col[:, cb:cb + 2 * KC], ALU.add).then_inc(mod_col_step, 1)
                dve.wait_ge(mod_col_step, v + 1)
                cn = COL_NORM + v * KC
                nc.vector.scalar_tensor_tensor(scale_col[:, :], mod_col[:, KC:2 * KC], 1.0, col[:, cn:cn + KC],
                                               ALU.add, ALU.mult).then_inc(mod_col_ready, 1)

            def pre_norm(v):
                for t in range(TT):
                    dve.wait_ge(rs_x_ready, 2 * v + t + 1)
                    nc.vector.tensor_scalar(tok[:, t, :], x[:, t, :], rs_x[:, t:t + 1], None, ALU.mult)\
                        .then_inc(xn_ready, 1)
                src = norm_bank(v)
                dve.wait_ge(mod_col_ready, v + 1)
                for k in range(KC):
                    dve.wait_ge(xt_done, KC * v + k + 1)
                    dve.wait_ge(h_ready, KC * v + k + 1)
                    nc.vector.tensor_copy(h_hi[:, k, :], feat_b[:, k, :]).then_inc(h_hi_ready, 1)

            def ffn_up(ffn):
                def body(b, s, r):
                    j = b - ffn["b"]
                    dve.wait_ge(side_ready, j + ffn["side"] + 1)
                    if not isinstance(j, int) or j >= SLOTS:
                        dve.wait_ge(act_lo_ready, j + (ffn["act"] - SLOTS + 1))
                    nc.vector.tensor_tensor(prod[:, s, :], side[:, s, :], up[:, s, SEQ:2 * SEQ], ALU.mult)\
                        .then_inc(prod_ready, 1)
                    prepare(b, s, r)
                each_block(dve, ffn["b"], ffn["up"], body)

            def lru(mix, li):
                c0 = COL_LRU + li * LRU_COLS

                def tap(k, n):
                    return col[:, c0 + k * KC + n:c0 + k * KC + n + 1]

                def body(b, s, r):
                    n = b - mix["b"]
                    src = up[:, s, SEQ:2 * SEQ]
                    dve.wait_ge(conv_ready, mix["conv"] + n + 1)
                    for m, (k, d) in enumerate(((0, 2), (1, 1), (3, -1))):
                        lo, hi = max(d, 0), SEQ + min(d, 0)
                        if m:
                            dve.wait_ge(conv_step, 2 * (KC * li + n) + m)
                        last = nc.vector.scalar_tensor_tensor(
                            feat_b[:, n, lo:hi], src[:, lo - d:hi - d], tap(k, n), feat_b[:, n, lo:hi],
                            ALU.mult, ALU.add)
                        last.then_inc(conv_step if m < 2 else up_free, 1)
                    dve.wait_ge(up_free, mix["q"] + n + 1)
                    nc.vector.tensor_copy(act_hi[:, n, :], feat_b[:, n, :]).then_inc(xc_hi_ready, 1)
                    prepare(b, s, r)
                straight(dve, mix["b"], mix["up"], body)
                for d in range(2):
                    for n in range(KC):
                        dve.wait_ge(gates_free, 2 * KC * li + KC * d + n + 1)
                        cs = (li * 2 + d) * KC + n
                        nc.vector.tensor_scalar(lru_r[d][:, n, :], lru_r[d][:, n, :], soft[:, 5, cs:cs + 1],
                                                None, ALU.mult).then_inc(y_ready, 1)
                    b = mix["b"] + mix["up"] + d
                    prepare(b, b % SLOTS, b // SLOTS)
                for d in range(2):
                    squared = (feat_a, feat_b)[d]
                    dve.wait_ge(decay_ready, 6 * li + 3 * d + 3)
                    nc.vector.scalar_tensor_tensor(lru_r[d][:, :, :], squared, 1.0, lru_r[d][:, :, :],
                                                   ALU.add, ALU.mult).then_inc(w_ready, 1)
                for d in range(2):
                    dve.wait_ge(root_ready, 2 * li + d + 1)
                    dve.wait_ge(ix_ready, 2 * KC * li + KC * (d + 1))
                    link(nc.vector.tensor_tensor(lru_r[d][:, :, :], lru_r[d][:, :, :], lru_i[d][:, :, :],
                                                 ALU.mult), 1)
                    step = 1 if d == 0 else -1
                    for n in range(KC):
                        last = nc.vector.tensor_tensor_scan(lru_i[d][:, n, ::step], lru_a[d][:, n, ::step],
                                                            lru_r[d][:, n, ::step], 0.0, ALU.mult, ALU.add)
                    link(last, 1)
                for n in range(KC):
                    last = nc.vector.tensor_tensor(lru_i[0][:, n, :], lru_i[0][:, n, :], lru_i[1][:, n, :], ALU.add)
                    link(last, 1)
                    nc.vector.tensor_tensor(feat_b[:, n, :], lru_i[0][:, n, :], feat_c[:, n, :], ALU.mult)\
                        .then_inc(prod_ready, 1)

            def attention(mix):
                def body(b, s, r):
                    n = b - mix["b"]
                    dve.wait_ge(q_ready, n + 1)
                    nc.vector.tensor_copy(feat_b[:, n, :], up[:, s, SEQ:2 * SEQ]).then_inc(up_free, 1)
                    prepare(b, s, r)
                straight(dve, mix["b"], mix["up"], body)
                straight(dve, mix["b"] + mix["up"], mix["mid"], prepare)
                dve.wait_ge(band_ready, 8)
                for h in range(HEADS + 3):
                    if h < HEADS:
                        dve.wait_ge(scores_done, h + 1)
                        wait(dve, pt_done, h - 3)
                        band = bands[h // 8][:, h % 8, :, :].rearrange("p j c -> p (j c)")
                        for t in range(TT):
                            j0 = (2 - 2 * t) * GRID_W
                            nc.vector.tensor_tensor_reduce(
                                out=probs[:, h % 4, t, :], in0=up[:, h % 2, t * SEQ:(t + 1) * SEQ],
                                in1=band[:, j0:j0 + SEQ], scale=1.0, scalar=-3e38, op0=ALU.add, op1=ALU.max,
                                accum_out=smax[:, h % 4, t:t + 1]).then_inc(score_ready, 1)
                        dve.wait_ge(score_ready, TT * (h + 1))
                        nc.vector.tensor_scalar(sneg[:, h % 4, :], smax[:, h % 4, :], -1.0, None, ALU.mult)\
                            .then_inc(neg_ready, 1)
                    if 1 <= h <= HEADS:
                        g = h - 1
                        dve.wait_ge(exp_ready, TT * (g + 1))
                        nc.vector.reciprocal(sinv[:, g % 4, :], ssum[:, g % 4, :]).then_inc(inv_ready, 1)
                        dve.wait_ge(inv_ready, g + 1)
                        for t in range(TT):
                            nc.vector.tensor_scalar(probs[:, g % 4, t, :], probs[:, g % 4, t, :],
                                                    sinv[:, g % 4, t:t + 1], None, ALU.mult)\
                                .then_inc(probs_ready, 1)
                    if h >= 4 and h % 2 == 0:
                        n = (h - 4) // 2
                        dve.wait_ge(act_hi_ready, mix["act"] + n + 1)
                        nc.vector.tensor_tensor(act_lo[:, n, :], down[:, (n % 4) // 2, n % 2, 0:SEQ],
                                                act_hi[:, n, :].bitcast(f32), ALU.subtract).then_inc(act_lo_ready, 1)

            def short_conv(mix):
                def pair(b, s, r):
                    n = b - mix["b"]
                    dve.wait_ge(side_ready, mix["side"] + n + 1)
                    nc.vector.tensor_tensor(feat_b[:, n, :], up[:, s, 0:SEQ], side[:, s, :], ALU.mult)\
                        .then_inc(up_free, 1)
                    prepare(b, s, r)
                    dve.wait_ge(conv_ready, mix["conv"] + n + 1)
                    for k, d in ((0, 1), (2, -1)):
                        lo, hi = max(d, 0), SEQ + min(d, 0)
                        w = col[:, COL_SC + k * KC + n:COL_SC + k * KC + n + 1]
                        link(nc.vector.scalar_tensor_tensor(
                            feat_c[:, n, lo:hi], feat_b[:, n, lo - d:hi - d], w, feat_c[:, n, lo:hi],
                            ALU.mult, ALU.add), 1)
                straight(dve, mix["b"], KC, pair)

                def gate(b, s, r):
                    j = b - mix["b"] - KC
                    dve.wait_ge(block_used, b + 1)
                    two = slice(2 * j * SEQ, (2 * j + 2) * SEQ)
                    nc.vector.tensor_tensor(buf_a[:, two], up[:, s, :], buf_c[:, two], ALU.mult)\
                        .then_inc(up_free, 1)
                    prepare(b, s, r)
                straight(dve, mix["b"] + KC, mix["up"] - KC, gate)

            nc.vector.memset(minus_half, -0.5).then_inc(consts_ready, 1)
            dve.wait_ge(cols_in, 16)
            lam = [soft[:, n, :] for n in range(6)]
            for li in range(N_LRU):
                c0 = COL_LRU + li * LRU_COLS + 9 * KC
                lam_col = col[:, c0:c0 + 2 * KC]
                last = nc.vector.scalar_tensor_tensor(lam[0][:, li * 2 * KC:(li + 1) * 2 * KC], lam_col, -1.0,
                                                      lam_col, ALU.mult, ALU.max)
            link(last)
            for li in range(N_LRU):
                c0 = COL_LRU + li * LRU_COLS + 9 * KC
                last = nc.vector.tensor_scalar(lam[5][:, li * 2 * KC:(li + 1) * 2 * KC], col[:, c0:c0 + 2 * KC],
                                               -1.0, 0.0, ALU.mult, ALU.max)
            link(last)
            dve.wait_ge(soft_exp, 1)
            link(nc.vector.tensor_scalar(lam[2], lam[1], 2.0, None, ALU.add))
            link(nc.vector.reciprocal(lam[3], lam[2]))
            link(nc.vector.tensor_tensor(lam[2], lam[1], lam[3], ALU.mult))
            link(nc.vector.tensor_tensor(lam[3], lam[2], lam[2], ALU.mult))
            terms = 9
            link(nc.vector.tensor_scalar(lam[4], lam[3], 2.0 / (2 * terms + 1), 2.0 / (2 * terms - 1), ALU.mult, ALU.add))
            for n in range(terms - 2, -1, -1):
                link(nc.vector.tensor_tensor(lam[4], lam[4], lam[3], ALU.mult))
                link(nc.vector.tensor_scalar(lam[4], lam[4], 2.0 / (2 * n + 1), None, ALU.add))
            link(nc.vector.tensor_tensor(lam[4], lam[4], lam[2], ALU.mult))
            link(nc.vector.tensor_tensor(lam[5], lam[5], lam[4], ALU.add))
            link(nc.vector.tensor_scalar(lam[5], lam[5], LRU_C, None, ALU.mult))

            dve.wait_ge(c_ready, 1)
            ada_block(0, ada_raw, ada_in, 16)
            for a in range(1, 4):
                ada_block(a, ada_extra[a - 1], ada_extra_in[a - 1], 16)
            ada_block(4, ada_raw, ada_in, 32)
            ada_block(5, ada_extra[0], ada_extra_in[0], 32)
            for b in range(SLOTS):
                lo_block(b, b)
            modulation(0)
            pre_norm(0)
            li = 0
            for i, (kind, mix, ffn) in enumerate(LAYERS):
                if kind == LRU:
                    lru(mix, li)
                    li += 1
                elif kind == ATTENTION:
                    attention(mix)
                else:
                    short_conv(mix)
                straight(dve, mix["out"], OUT_BLOCKS - 1, prepare)
                modulation(2 * i + 1)
                post_norm(2 * i)
                pre_norm(2 * i + 1)
                straight(dve, mix["end"] - 1, 1, prepare)
                ada_in_loop[0] = ada_after(ffn["end"] - 1 - (ffn["end"] % SLOTS)) is not None
                ffn_up(ffn)
                each_block(dve, ffn["out"], min(FFN_DOWN - 1, BLOCKS - SLOTS - ffn["out"]), prepare)
                if i < DEPTH - 1:
                    modulation(2 * i + 2)
                post_norm(2 * i + 1)
                if i < DEPTH - 1:
                    pre_norm(2 * i + 2)
                    straight(dve, ffn["end"] - 1, 1, prepare)

        @block.gpsimd
        def _(pool):
            counts = {"rs": 0}

            def inverse_rms(sums, t, dst, ready):
                nc.gpsimd.tensor_tensor(tmp[:, 0:1], sums[:, 2 * t:2 * t + 1], sums[:, 2 * t + 1:2 * t + 2],
                                        ALU.add).then_inc(rs_step, 1)
                pool.wait_ge(rs_step, counts["rs"] + 1)
                nc.gpsimd.tensor_scalar(tmp[:, 1:2], tmp[:, 0:1], 1.0 / D_MODEL, EPS, ALU.mult, ALU.add)\
                    .then_inc(rs_step, 1)
                pool.wait_ge(rs_step, counts["rs"] + 2)
                nc.gpsimd.tensor_tensor(dst[:, t:t + 1], tmp[:, 1:2], minus_half, ALU.pow).then_inc(ready, 1)
                counts["rs"] += 2

            def sum_ada(a):
                pool.wait_ge(acc_ready, a + 1)
                wait(pool, mod_out, a * 16)
                pool.sem_inc(sum_turn, 1)
                nc.gpsimd.partition_all_reduce(ada_sum[:, :], ada_acc[:, :], P, bass.bass_isa.ReduceOp.add)\
                    .then_inc(acc_free, 1)
                pool.wait_ge(acc_free, a + 1)
                pool.dma_start(mod_rows[a], ada_sum[0:1, :]).then_inc(mod_out, 16)

            def mod_at(i, group, rows):
                off = (6 * i + group) * D_MODEL
                return off, -(-(off + rows * P) // ADA_COLS)

            def load_mod_row(v):
                i, part = divmod(v, 2)
                off, n = mod_at(i, 3 * part, 2 * KC)
                pool.wait_ge(mod_out, 16 * n)
                wait(pool, mod_t_done, v)
                pool.dma_start(mod_row[:, :], bass.AP(mod_dram, off, [[P, 2 * KC], [1, P]]))\
                    .then_inc(mod_row_in, 16)

            def load_gate_row(u):
                i, part = divmod(u, 2)
                group = 3 * part + 2
                off, n = mod_at(i, group, KC)
                pool.wait_ge(mod_out, 16 * n)
                wait(pool, x_ready, 4 * u)
                every = [[0, P], [1, D_MODEL]]
                pool.dma_start(gate_row[:, :], bass.AP(mod_dram, off, every)).then_inc(rows_in, 16)
                pool.dma_start(bias_row[:, :], bass.AP(ada_b.tensor, (6 * i + group) * D_MODEL, every))\
                    .then_inc(rows_in, 16)
                pool.dma_start(norm_row[:, :], bass.AP(norm_g.tensor, (4 * i + 2 * part + 1) * D_MODEL, every))\
                    .then_inc(rows_in, 16)
                pool.wait_ge(rows_in, 48 * (u + 1))
                nc.gpsimd.tensor_tensor(gate_row[:, :], gate_row[:, :], bias_row[:, :], ALU.add).then_inc(rs_step, 1)
                counts["rs"] += 1
                pool.wait_ge(rs_step, counts["rs"])
                nc.gpsimd.tensor_tensor(gate_row[:, :], gate_row[:, :], norm_row[:, :], ALU.mult)\
                    .then_inc(gate_row_ready, 1)

            def behind(b, s, r):
                if isinstance(b, int):
                    if ada_after(b) is not None:
                        sum_ada(ada_after(b))
                elif s == SLOTS - 1 and ada_in_loop[0]:
                    sum_ada(r + 11)

            ada_in_loop = [True]

            def norms(u, v):
                if u is not None:
                    for t in range(TT):
                        pool.wait_ge(sq_m_ready, 4 * u + 2 * t + 2)
                        inverse_rms(sq_m, t, rs_m, rs_m_ready)
                if v is not None:
                    for t in range(TT):
                        pool.wait_ge(sq_x_ready, 4 * v + 2 * t + 2)
                        inverse_rms(sq_x, t, rs_x, rs_x_ready)
                    for k in range(KC):
                        pool.wait_ge(h_hi_ready, KC * v + k + 1)
                        nc.gpsimd.tensor_tensor(h_lo[:, k, :], feat_b[:, k, :], h_hi[:, k, :].bitcast(f32),
                                                ALU.subtract).then_inc(h_lo_ready, 1)

            def act_low(n, src, base):
                pool.wait_ge(act_hi_ready, n + (base + 1))
                nc.gpsimd.tensor_tensor(act_lo[:, n, :], src, act_hi[:, n, :].bitcast(f32), ALU.subtract)\
                    .then_inc(act_lo_ready, 1)

            def out_phase(u, first, n):
                each_block(pool, first, n - 4, behind)
                for b in range(first + n - 4, first + n):
                    if b == first + n - 4:
                        load_gate_row(u)
                    if b == first + n - 2 and u + 1 < 2 * DEPTH:
                        load_mod_row(u + 1)
                    if b < first + n - 1:
                        behind(b, b % SLOTS, b // SLOTS)
                norms(u, u + 1 if u + 1 < 2 * DEPTH else None)
                b = first + n - 1
                behind(b, b % SLOTS, b // SLOTS)

            def lru(mix, li):
                def body(b, s, r):
                    n = b - mix["b"]
                    pool.wait_ge(xc_hi_ready, KC * li + n + 1)
                    nc.gpsimd.tensor_tensor(act_lo[:, n, :], feat_b[:, n, :], act_hi[:, n, :].bitcast(f32),
                                            ALU.subtract).then_inc(xc_lo_ready, 1)
                    behind(b, s, r)
                straight(pool, mix["b"], mix["up"], body)
                for d in range(2):
                    for n in range(KC):
                        pool.wait_ge(gates_free, 2 * KC * li + KC * d + n + 1)
                        nc.gpsimd.tensor_tensor(lru_i[d][:, n, :], lru_i[d][:, n, :], feat_b[:, n, :], ALU.mult)\
                            .then_inc(ix_ready, 1)
                    b = mix["b"] + mix["up"] + d
                    behind(b, b % SLOTS, b // SLOTS)
                for n in range(KC):
                    act_low(n, feat_b[:, n, :], mix["act"])

            def attention(mix):
                pool.wait_ge(band_in, 16 * 4 * BAND)
                for half in range(2):
                    for rl in range(2):
                        part = bands[half][rl * GRID_W:(rl + 1) * GRID_W, :, :, :].rearrange("p h j c -> p (h j) c")
                        rows = HEADS // 2 * BAND
                        low, high = part[:, :, 0:48], part[:, :, 16:GRID_W]
                        nc.gpsimd.affine_select(out=low, in_=low, compare_op=ALU.is_ge, fill=NEG, base=8 - (GRID_W - 1),
                                                pattern=[[0, rows], [1, 48]], channel_multiplier=1)\
                            .then_inc(band_ready, 1)
                        pool.wait_ge(band_ready, 4 * half + 2 * rl + 1)
                        nc.gpsimd.affine_select(out=high, in_=high, compare_op=ALU.is_ge, fill=NEG, base=GRID_W - 1 + 7 - 16,
                                                pattern=[[0, rows], [-1, 48]], channel_multiplier=-1)\
                            .then_inc(band_ready, 1)
                pool.wait_ge(band_ready, 8)
                straight(pool, mix["b"], mix["up"] + mix["mid"], behind)

            def short_conv(mix):
                straight(pool, mix["b"], KC, behind)

                def gate(b, s, r):
                    j = b - mix["b"] - KC
                    for n in (2 * j, 2 * j + 1):
                        act_low(n, feat_a[:, n, :], mix["act"])
                    behind(b, s, r)
                straight(pool, mix["b"] + KC, mix["up"] - KC, gate)

            def ffn_up(ffn):
                def body(b, s, r):
                    act_low(b - ffn["b"], prod[:, s, :], ffn["act"])
                    behind(b, s, r)
                each_block(pool, ffn["b"], ffn["up"], body)

            nc.gpsimd.memset(ident[:, :], 0.0).then_inc(ident_ready, 1)
            pool.wait_ge(ident_ready, 1)
            nc.gpsimd.affine_select(out=ident[:, :], in_=ident[:, :], compare_op=ALU.not_equal, fill=1.0,
                                    base=0, pattern=[[-1, P]], channel_multiplier=1).then_inc(ident_ready, 1)
            pool.wait_ge(consts_ready, 1)
            for a in range(ADA_FIRST):
                sum_ada(a)
            load_mod_row(0)
            norms(None, 0)
            li = 0
            for i, (kind, mix, ffn) in enumerate(LAYERS):
                if kind == LRU:
                    lru(mix, li)
                    li += 1
                elif kind == ATTENTION:
                    attention(mix)
                else:
                    short_conv(mix)
                out_phase(2 * i, mix["out"], OUT_BLOCKS)
                ada_in_loop[0] = ada_after(ffn["end"] - 1 - (ffn["end"] % SLOTS)) is not None
                ffn_up(ffn)
                out_phase(2 * i + 1, ffn["out"], FFN_DOWN)


def _counts():
    side = prod = conv = 0
    for kind, mix, ffn in LAYERS:
        mix.update(side=side, prod=prod, conv=conv)
        if kind == SHORT_CONV:
            side += KC
        if kind == LRU:
            prod += KC
        if kind != ATTENTION:
            conv += KC
        ffn.update(side=side, prod=prod)
        side += FC
        prod += FC


_counts()


def _up_blocks(wa, wb):
    n = wa.shape[1] // P
    both = np.stack([w.reshape(KC, P, n, P) for w in (wa, wb)])
    return both.transpose(3, 2, 1, 0, 4).reshape(n, P, BLOCK)


def _down_blocks(w):
    return w.reshape(-1, 2, P, D_MODEL).transpose(0, 2, 1, 3).reshape(-1, P, BLOCK)


def _columns(v):
    return np.ascontiguousarray(v.reshape(-1, P).T)


def kernel(x, c, ada_w, ada_b, norm_g, ffn_w_gu, ffn_w_down,
           lru_w_in, lru_conv_w, lru_conv_b, lru_gate_w, lru_gate_b, lru_lambda, lru_w_out,
           na_w_qkv, na_rpb, na_w_o, sc_w_in, sc_conv_w, sc_w_out):
    import concourse.bacc as bacc
    from concourse.bass_utils import run_bass_kernel_spmd

    D = D_MODEL
    blocks = []
    for i, kind in enumerate(KINDS):
        j = i // 3
        if kind == LRU:
            w = np.asarray(lru_w_in[j])
            blocks.append(_up_blocks(w[:, :D], w[:, D:]))
            blocks.append(np.asarray(lru_gate_w[j]).transpose(0, 3, 2, 1, 4).reshape(2, P, BLOCK))
            blocks.append(_down_blocks(np.asarray(lru_w_out[j])))
        elif kind == ATTENTION:
            w = np.asarray(na_w_qkv[j])
            blocks.append(_up_blocks(w[:, :D], w[:, D:2 * D]))
            blocks.append(_down_blocks(np.ascontiguousarray(w[:, 2 * D:])))
            blocks.append(_down_blocks(np.asarray(na_w_o[j])))
        else:
            w = np.asarray(sc_w_in[j])
            blocks.append(_up_blocks(w[:, D:2 * D], w[:, 2 * D:]))
            b_gate = w[:, :D].reshape(D, KC // 2, 2, P)
            blocks.append(_up_blocks(b_gate[:, :, 0].reshape(D, D // 2), b_gate[:, :, 1].reshape(D, D // 2)))
            blocks.append(_down_blocks(np.asarray(sc_w_out[j])))
        w = np.asarray(ffn_w_gu[i])
        blocks.append(_up_blocks(w[:, :FFN_HIDDEN], w[:, FFN_HIDDEN:]))
        blocks.append(_down_blocks(np.asarray(ffn_w_down[i])))
    stream = np.concatenate(blocks)
    ada = np.asarray(ada_w).reshape(DEPTH, KC, P, 6 * D // ADA_COLS, ADA_COLS)
    ada = np.ascontiguousarray(ada.transpose(0, 3, 2, 1, 4).reshape(ADA_BLOCKS, P, KC * ADA_COLS))
    norm = np.asarray(norm_g)
    parts = [_columns(np.asarray(c)), _columns(np.asarray(ada_b)),
             _columns(np.ascontiguousarray(norm[:, 0::2]))]
    for li in range(N_LRU):
        parts += [_columns(np.asarray(a[li])) for a in (lru_conv_w, lru_conv_b, lru_gate_b, lru_lambda)]
    parts.append(_columns(np.asarray(sc_conv_w)))
    arrays = {
        "stream": stream, "ada": ada, "cols": np.concatenate(parts, axis=1),
        "x_in": np.asarray(x).reshape(SEQ, D), "norm": norm.reshape(-1), "ada_bias": np.asarray(ada_b).reshape(-1),
        "rpb_flat": np.asarray(na_rpb).reshape(-1),
    }
    nc = bacc.Bacc("TRN2", target_bir_lowering=False, num_devices=1)
    args = []
    for name, a in arrays.items():
        arrays[name] = np.ascontiguousarray(a)
        args.append(nc.dram_tensor(name, a.shape, mybir.dt.from_np(a.dtype), kind="ExternalInput").ap())
    out = nc.dram_tensor("out", (SEQ, D), mybir.dt.float32, kind="ExternalOutput").ap()
    encoder(nc, *args, out)
    r = run_bass_kernel_spmd(nc, [arrays], core_ids=[0])
    return r.results[0]["out"].reshape(1, SEQ, D)
```

```python
import concourse.bass as bass
import numpy as np
from concourse import mybir
from concourse.alu_op_type import AluOpType as ALU
from contextlib import ExitStack

P = 128
D_MODEL, SEQ, DEPTH = 1024, 256, 4
KC = D_MODEL // P
TT = SEQ // P
HALF = 512
FFN_HIDDEN = 2816
FC = FFN_HIDDEN // P
EPS = 1e-6
ROOT_MEAN = D_MODEL ** -0.5
LRU_C = 8.0
HEADS, HEAD_DIM = 16, 64
GRID_W, ROWS = 64, 4
RPB_ROWS, RPB_COLS = 15, 31
BAND = 6
BAND_RUN = (BAND - 1) * RPB_COLS + GRID_W
NEG = -1e30

BLOCK = 2048
SLOTS = 3
LRU, ATTENTION, SHORT_CONV = 0, 1, 2
GROUP = KC // 2
KINDS = [i % 3 for i in range(DEPTH)]
MIX_UP = {LRU: 8, ATTENTION: 8, SHORT_CONV: 12}
MIX_MID = {LRU: 2, ATTENTION: 4, SHORT_CONV: 0}
OUT_BLOCKS = D_MODEL // (2 * P)
FFN_DOWN = FC // 2

ADA_COLS = 384
ADA_BLOCKS = DEPTH * 6 * D_MODEL // ADA_COLS
HEAD_ALONE = (0, 1, 2, 14, 15)
ADA_HEAD = 2 * D_MODEL // ADA_COLS


def _layout():
    layers, b, q, act, split_norms = [], 0, 0, 0, 0
    for i, kind in enumerate(KINDS):
        mix = dict(b=b, q=q, act=act, split_norms=split_norms, up=MIX_UP[kind], mid=MIX_MID[kind])
        mix["out"] = b + mix["up"] + mix["mid"]
        b, q = mix["out"] + OUT_BLOCKS, q + mix["up"]
        if kind != LRU:
            act, split_norms = act + KC, split_norms + 1
        ffn = dict(b=b, act=act, split_norms=split_norms, up=FC)
        act, split_norms = act + FC, split_norms + 1
        ffn["out"] = b + FC
        b = ffn["out"] + FFN_DOWN
        mix["end"], ffn["end"] = ffn["b"], b
        layers.append((kind, mix, ffn))
    return layers, b


LAYERS, BLOCKS = _layout()
ROUNDS = BLOCKS // SLOTS


def lru_block(mix, n):
    return mix["b"] + n + n // GROUP


def lru_gates(mix, g):
    return mix["b"] + (GROUP + 1) * g + GROUP


def plain(b):
    return any(kind == LRU and mix["b"] <= b < mix["end"] for kind, mix, _ in LAYERS)


def splits(b, lrus):
    if isinstance(b, int):
        return sum(not plain(m) for m in range(b + 1))
    return b + (1 - lrus * (MIX_UP[LRU] + MIX_MID[LRU] + OUT_BLOCKS))


EARLY_AT = (0, 1, 2, 3, 5, 6, 7, 8, 11)
EARLY = 8
EARLY_SLOTS = 4


def ada_after(b):
    if b <= EARLY_AT[-1]:
        return ADA_HEAD + 1 + EARLY_AT.index(b) if b in EARLY_AT else None
    r, s = divmod(b, SLOTS)
    return r + 11 if s == 2 and r + 11 < ADA_BLOCKS else None


COL_C = 0
COL_ADA_B = COL_C + KC
COL_NORM = COL_ADA_B + DEPTH * 6 * KC
COL_LRU = COL_NORM + DEPTH * 2 * KC
LRU_COLS = (4 + 1 + 4 + 2) * KC
N_LRU = KINDS.count(LRU)
COL_SC = COL_LRU + N_LRU * LRU_COLS
COLS = COL_SC + 3 * KC


def encoder(nc, stream, ada, cols, x_in, norm_g, ada_b, rpb, out):
    f32, f32r, bf16 = mybir.dt.float32, mybir.dt.float32r, mybir.dt.bfloat16
    ACT = mybir.ActivationFunctionType
    ctx = ExitStack()
    with ctx:
        def sb(name, shape, dtype=f32):
            return ctx.enter_context(nc.sbuf_tensor(name, shape, dtype))

        def sem(name):
            return ctx.enter_context(nc.semaphore(name))

        base = -(-nc.sbuf_base // 32) * 32
        h_hi = sb("h_hi", [P, KC, SEQ], f32r)
        h_lo = sb("h_lo", [P, KC, SEQ], f32r)
        act_hi = sb("act_hi", [P, FC, SEQ], f32r)
        act_lo = sb("act_lo", [P, FC, SEQ], f32r)
        chunk = SEQ * 4
        at_h_lo, at_act_hi = base + KC * chunk, base + 2 * KC * chunk
        at_act_lo = at_act_hi + FC * chunk

        def over(name, shape, offset):
            return nc.alloc_sbuf_tensor_at(name, shape, f32, offset=offset)

        h_plain = over("h_plain", [P, KC, SEQ], base)
        wide = [P, 2, GROUP, SEQ]
        lru_r = [over("lru_r0", wide, at_act_hi + KC * chunk), over("lru_r1", wide, base)]
        lru_i = [over("lru_i0", wide, at_act_lo + KC * chunk), over("lru_i1", wide, at_h_lo)]
        lru_a1 = over("lru_a1", wide, at_act_hi + KC * chunk)
        both_acts = over("both_acts", [P, 2, FC, SEQ], at_act_hi)
        lru_sq = both_acts[:, :, 2 * KC:2 * KC + GROUP, :]
        bands = [over("band0", [P, HEADS // 2, BAND, GRID_W], at_act_hi + KC * chunk),
                 over("band1", [P, HEADS // 2, BAND, GRID_W], at_act_lo + KC * chunk)]
        band_runs = [over("band_run0", [P, HEADS // 2, BAND_RUN], at_act_hi),
                     over("band_run1", [P, HEADS // 2, BAND_RUN], at_act_lo)]
        probs = over("probs", [P, 4, TT, SEQ], base)
        probs_t = over("probs_t", [P, 4, TT, SEQ], at_h_lo)
        ada_head = [over(f"ada_head{i}", [P, KC, ADA_COLS], base + i * KC * ADA_COLS * 4)
                    for i in range(ADA_HEAD)]
        at_w_hi = base + (2 * KC + 2 * FC) * chunk + SLOTS * BLOCK * 4
        ada_early = [over(f"ada_early{i}", [P, KC, ADA_COLS],
                          at_w_hi + i // 2 * SLOTS * BLOCK * 4 + i % 2 * KC * ADA_COLS * 4)
                     for i in range(EARLY_SLOTS)]

        raw = sb("raw", [P, SLOTS, BLOCK])
        w_hi = sb("w_hi", [P, SLOTS, BLOCK], f32r)
        w_lo = sb("w_lo", [P, SLOTS, BLOCK], f32r)
        ada_raw = sb("ada_raw", [P, KC, ADA_COLS])
        ada_acc = sb("ada_acc", [P, ADA_COLS])
        ada_sum = sb("ada_sum", [P, 2, ADA_COLS])
        x = sb("x", [P, TT, D_MODEL])
        buf_a = sb("buf_a", [P, KC * SEQ])
        buf_b = sb("buf_b", [P, KC * SEQ])
        buf_c = sb("buf_c", [P, KC * SEQ])
        tok = buf_a[:, :].rearrange("p (t d) -> p t d", t=TT)
        feat_a = buf_a[:, :].rearrange("p (k s) -> p k s", k=KC)
        feat_b = buf_b[:, :].rearrange("p (k s) -> p k s", k=KC)
        feat_c = buf_c[:, :].rearrange("p (k s) -> p k s", k=KC)
        lru_a = [buf_a[:, :].rearrange("p (d n s) -> p d n s", d=2, n=GROUP), lru_a1]
        values = buf_c[:, :].rearrange("p (t d) -> p t d", t=TT)
        gate_row = sb("gate_row", [P, D_MODEL])
        bias_row = sb("bias_row", [P, D_MODEL])
        norm_row = sb("norm_row", [P, D_MODEL])
        side = sb("side", [P, SLOTS, SEQ])
        prod = sb("prod", [P, SLOTS, SEQ])
        junk = sb("junk", [P, 4, HALF], bf16)
        col = sb("col", [P, COLS])
        c_act = sb("c_act", [P, KC])
        mod_row = sb("mod_row", [2 * KC, P])
        mod_col = sb("mod_col", [P, 2 * KC])
        scale_col = sb("scale_col", [P, KC])
        lam_n = N_LRU * 2 * KC
        soft = sb("soft", [P, 6, lam_n])
        stat = sb("stat", [P, 24])
        sq_m, sq_x, rs_m, rs_x, part = (stat[:, c:c + n] for c, n in
                                        ((0, 4), (4, 4), (8, TT), (10, TT), (12, TT)))
        minus_half, ones = stat[:, 14:15], stat[:, 15:16]
        smax = sb("smax", [P, 4, TT])
        sneg = sb("sneg", [P, 4, TT])
        ssum = sb("ssum", [P, 4, TT])
        sinv = sb("sinv", [P, 4, TT])
        ident = sb("ident", [P, P])

        up = ctx.enter_context(nc.psum_tensor("up", [P, 4, HALF], f32))
        down = ctx.enter_context(nc.psum_tensor("down", [P, TT, 2, HALF], f32))
        mod_dram = nc.dram_tensor("mod_scratch", [ADA_BLOCKS, ADA_COLS], f32)
        mod_rows = mod_dram.ap().rearrange("a (o c) -> a o c", o=1)

        raw_in = [sem(f"raw_in{s}") for s in range(SLOTS)]
        hi_ready, lo_ready, block_used = sem("hi_ready"), sem("lo_ready"), sem("block_used")
        cols_in, x_loaded = sem("cols_in"), sem("x_loaded")
        ada_in, ada_head_in = sem("ada_in"), [sem(f"ada_head_in{i}") for i in range(ADA_HEAD + 1)]
        ada_early_in = [sem(f"ada_early_in{i}") for i in range(EARLY_SLOTS)]
        head_step, head_ready = sem("head_step"), sem("head_ready")
        acc_step, acc_ready, acc_free = sem("acc_step"), sem("acc_ready"), sem("acc_free")
        early_out = [sem(f"early_out{i}") for i in range(2)]
        mod_out, mod_row_in, rows_in = sem("mod_out"), sem("mod_row_in"), sem("rows_in")
        mod_t_done, mod_col_step, mod_col_ready = sem("mod_t_done"), sem("mod_col_step"), sem("mod_col_ready")
        sum_turn = sem("sum_turn")
        gate_sum_ready, gate_row_ready = sem("gate_sum_ready"), sem("gate_row_ready")
        ident_ready, consts_ready, c_ready = sem("ident_ready"), sem("consts_ready"), sem("c_ready")
        soft_exp, soft_step = sem("soft_exp"), sem("soft_step")
        sq_m_ready, sq_x_ready = sem("sq_m_ready"), sem("sq_x_ready")
        part_ready, rs_m_ready, rs_x_ready = sem("part_ready"), sem("rs_m_ready"), sem("rs_x_ready")
        delta_ready, x_ready, xn_ready, xn_act_ready = (
            sem("delta_ready"), sem("x_ready"), sem("xn_ready"), sem("xn_act_ready"))
        xt_done, h_ready, h_hi_ready, h_lo_even, h_lo_odd = (
            sem("xt_done"), sem("h_ready"), sem("h_hi_ready"), sem("h_lo_even"), sem("h_lo_odd"))
        up_free, down_done = sem("up_free"), sem("down_done")
        side_ready = sem("side_ready")
        prod_ready, act_hi_ready, act_lo_ready = sem("prod_ready"), sem("act_hi_ready"), sem("act_lo_ready")
        conv_ready, conv_step = sem("conv_ready"), sem("conv_step")
        gates_done, gates_free, y_ready, ix_ready = sem("gates_done"), sem("gates_free"), sem("y_ready"), sem("ix_ready")
        scans_done = sem("scans_done")
        decay_ready, w_ready, root_ready, vector_step = sem("decay_ready"), sem("w_ready"), sem("root_ready"), sem("vector_step")
        q_ready, v_done, v_ready, band_spread, band_ready = sem("q_ready"), sem("v_done"), sem("v_ready"), sem("band_spread"), sem("band_ready")
        band_in = [sem(f"band_in{half}") for half in range(2)]
        scores_done, score_ready, neg_ready, exp_ready = sem("scores_done"), sem("score_ready"), sem("neg_ready"), sem("exp_ready")
        inv_ready, probs_ready, pt_done, pt_ready, pv_done = sem("inv_ready"), sem("probs_ready"), sem("pt_done"), sem("pt_ready"), sem("pv_done")
        stored = sem("stored")

        block = ctx.enter_context(nc.Block())

        def wait(eng, s, value):
            if not isinstance(value, int) or value > 0:
                eng.wait_ge(s, value)

        def each_block(eng, first, n, body):
            b, end = first, first + n
            while b < end and (b % SLOTS or b < SLOTS):
                body(b, b % SLOTS, b // SLOTS)
                b += 1
            rounds = (end - b) // SLOTS
            if rounds > 1:
                with eng.Fori(b // SLOTS, b // SLOTS + rounds) as r:
                    for s in range(SLOTS):
                        body(r * SLOTS + s, s, r)
                b += rounds * SLOTS
            while b < end:
                body(b, b % SLOTS, b // SLOTS)
                b += 1

        def straight(eng, first, n, body):
            for b in range(first, first + n):
                body(b, b % SLOTS, b // SLOTS)

        def quarters():
            for n in range(4):
                yield n, n // 2, n % 2, slice((n % 2) * HALF, (n % 2 + 1) * HALF)

        def norm_bank(v):
            s = first_slot(v)
            banks = [up[:, 3, :], up[:, (s + 1) % SLOTS, :], up[:, (s + 2) % SLOTS, :], down[:, 0, 0, :]]
            return [banks[k // 2][:, (k % 2) * SEQ:(k % 2 + 1) * SEQ] for k in range(KC)]

        def first_slot(v):
            return LAYERS[v // 2][1 + v % 2]["b"] % SLOTS

        @block.sync
        def _(sp):
            lrus = [1]

            def load(m, s):
                if isinstance(m, int) and m >= SLOTS and plain(m - SLOTS):
                    sp.wait_ge(block_used, m - SLOTS + 1)
                elif not isinstance(m, int) or m >= SLOTS:
                    sp.wait_ge(lo_ready, splits(m - SLOTS, lrus[0]))
                sp.dma_start(raw[:, s, :], stream[m]).then_inc(raw_in[s], 16)

            def load_ada(a):
                wait(sp, acc_ready, a - ADA_HEAD)
                sp.dma_start(ada_raw[:, :, :], ada[a]).then_inc(ada_in, 16)

            sp.dma_start(col[:, :], cols).then_inc(cols_in, 16)
            for t in range(TT):
                sp.dma_start(x[:, t, :], x_in[t * P:(t + 1) * P, :]).then_inc(x_loaded, 16)
            for a in range(ADA_HEAD):
                sp.dma_start(ada_head[a][:, :, :], ada[a]).then_inc(ada_head_in[a], 16)
            by_chunk = ada[ADA_HEAD].rearrange("p (k c) -> p k c", k=KC)
            sp.dma_start(ada_raw[:, :, 0:P], by_chunk[:, :, 0:P]).then_inc(ada_head_in[ADA_HEAD], 16)
            for s in range(SLOTS - 1):
                load(s, s)
            sp.dma_start(ada_raw[:, :, P:], by_chunk[:, :, P:]).then_inc(ada_in, 16)
            load(SLOTS - 1, SLOTS - 1)
            def load_early(a):
                i = (a - ADA_HEAD - 1) % EARLY_SLOTS
                if a > ADA_HEAD + EARLY_SLOTS:
                    sp.wait_ge(acc_ready, a - EARLY_SLOTS - ADA_HEAD + 1)
                sp.dma_start(ada_early[i][:, :, :], ada[a]).then_inc(ada_early_in[i], 16)

            for i in range(EARLY_SLOTS):
                load_early(ADA_HEAD + 1 + i)

            def load_both(m):
                load(m, m % SLOTS)
                first = ADA_HEAD + 1 + EARLY
                if m - SLOTS - 2 in range(EARLY - EARLY_SLOTS):
                    load_early(first - (EARLY - EARLY_SLOTS) + m - SLOTS - 2)
                if m == EARLY:
                    sp.wait_ge(mod_t_done, 1)
                    sp.wait_ge(acc_ready, 1)
                    sp.dma_start(ada_raw[:, :, :], ada[first]).then_inc(ada_in, 16)
                for b in (m - 2 * SLOTS, m - SLOTS - 1):
                    if b < 0 or ada_after(b) in (None, ADA_BLOCKS - 1) or ada_after(b) < first:
                        continue
                    if b == m - (SLOTS + 1 if plain(b + 2) else 2 * SLOTS):
                        load_ada(ada_after(b) + 1)

            for m in range(SLOTS, 7 * SLOTS):
                load_both(m)
            last_lru = LAYERS[-1][1]
            assert last_lru["end"] // SLOTS < ADA_BLOCKS - 10
            with sp.Fori(7, last_lru["b"] // SLOTS + 1) as r:
                for s in range(SLOTS):
                    load(r * SLOTS + s, s)
                load_ada(r + 10)
            for r in range(last_lru["b"] // SLOTS + 1, ADA_BLOCKS - 10):
                for s in range(SLOTS):
                    load_both(r * SLOTS + s)
            lrus[0] += 1
            with sp.Fori(ADA_BLOCKS - 10, ROUNDS) as r:
                for s in range(SLOTS):
                    load(r * SLOTS + s, s)
            for t in range(TT):
                sp.wait_ge(x_ready, 4 * (2 * DEPTH - 1) + 2 * (t + 1))
                sp.dma_start(out[t * P:(t + 1) * P, :], x[:, t, :]).then_inc(stored, 16)
            sp.wait_ge(stored, 16 * TT)

        @block.tensor
        def _(pe):
            def three(dst, w, act_of, k, cols_w, cols_a, weights_stationary, start, stop, check=False):
                hi_a, lo_a = act_of
                terms = ((w_hi, hi_a), (w_hi, lo_a), (w_lo, hi_a))
                for n, (wt, at) in enumerate(terms):
                    wv, av = wt[:, w, cols_w], at[:, k, cols_a]
                    lhs, rhs = (wv, av) if weights_stationary else (av, wv)
                    last = nc.tensor.matmul(dst, lhs, rhs, start=start and n == 0, stop=stop and n == 2,
                                            skip_group_check=check)
                return last

            def first_modulation(columns):
                for j in columns:
                    a, m = divmod(j, ADA_COLS // P)
                    src = ada_head[a] if a < ADA_HEAD else ada_raw
                    if j in HEAD_ALONE:
                        pe.wait_ge(ada_head_in[a], 16)
                    else:
                        pe.wait_ge(head_ready, a)
                    for k in range(KC if j in HEAD_ALONE else 1):
                        rhs = c_act[:, k:k + 1] if j in HEAD_ALONE else ones
                        last = nc.tensor.matmul(up[:, first_slot(0), j:j + 1], src[:, k, m * P:(m + 1) * P],
                                                rhs, start=k == 0, stop=k == (KC if j in HEAD_ALONE else 1) - 1)
                return last

            def transpose_modulation(v):
                pe.wait_ge(mod_row_in, 16 * v)
                nc.tensor.transpose(up[:, first_slot(v), 0:2 * KC], mod_row[:, :], ident[0:2 * KC, 0:2 * KC])\
                    .then_inc(mod_t_done, 1)

            def transposes(v):
                dst = norm_bank(v)
                for t in range(TT):
                    pe.wait_ge(xn_ready, 2 * v + t + 1)
                    for k in range(KC):
                        if t == TT - 1 and k == KC // 2:
                            pe.wait_ge(xn_act_ready, v + 1)
                        last = nc.tensor.transpose(dst[k][:, t * P:(t + 1) * P],
                                                   tok[:, t, k * P:(k + 1) * P], ident[:, :])
                        if t == TT - 1:
                            last.then_inc(xt_done, 1)
                    if t == 0 and v > 0:
                        transpose_modulation(v)

            lrus = [0]

            def up_phase(norms, b0, n, free, q0):
                def body(b, s, r):
                    pe.wait_ge(lo_ready, splits(b, lrus[0]))
                    first = isinstance(b, int) and b == b0
                    if isinstance(b, int):
                        wait(pe, free, q0 + max(b - b0 - 2, 0))
                    else:
                        pe.wait_ge(free, b + (q0 - b0 - 2))
                    for k in range(KC):
                        if first:
                            pe.wait_ge((h_lo_even, h_lo_odd)[k % 2], KC // 2 * norms + k // 2 + 1)
                        for o in range(2):
                            c0 = (2 * k + o) * P
                            last = three(up[:, s, o * SEQ:(o + 1) * SEQ], s, (h_hi, h_lo), k,
                                         slice(c0, c0 + P), slice(0, SEQ), True,
                                         start=k == 0 and o == 0, stop=k == KC - 1, check=True)
                    last.then_inc(block_used, 1)
                body(b0, b0 % SLOTS, b0 // SLOTS)
                each_block(pe, b0 + 1, n - 1, body)

            def down_phase(acts, b0, n, act_base, done, chunks_ready):
                for j in range(n):
                    b = b0 + j
                    s = b % SLOTS
                    pe.wait_ge(lo_ready, splits(b, lrus[0]))
                    if chunks_ready is not None:
                        pe.wait_ge(chunks_ready, act_base + 2 * j + 2)
                    for t in range(TT):
                        for h in range(2):
                            for kk in range(2):
                                c0 = kk * D_MODEL + h * HALF
                                last = three(down[:, t, h, :], s, acts, 2 * j + kk,
                                             slice(c0, c0 + HALF), slice(t * P, (t + 1) * P), False,
                                             start=j == 0 and kk == 0, stop=j == n - 1 and kk == 1)
                            if j == n - 1 and (t, h) != (TT - 1, 1):
                                last.then_inc(done, 1)
                    last.then_inc(block_used, 1)

            def lru(v, mix, li):
                def loaded(b):
                    pe.wait_ge(raw_in[b % SLOTS], 16 * (b // SLOTS + 1))

                for n in range(KC):
                    b = lru_block(mix, n)
                    loaded(b)
                    wait(pe, up_free, mix["q"] + sum(lru_block(mix, m) <= b - SLOTS for m in range(KC)))
                    for k in range(KC):
                        if n == 0:
                            pe.wait_ge(h_ready, KC * v + k + 1)
                        for o in range(2):
                            c0 = (2 * k + o) * P
                            last = nc.tensor.matmul(up[:, b % SLOTS, o * SEQ:(o + 1) * SEQ],
                                                    raw[:, b % SLOTS, c0:c0 + P], h_plain[:, k, :],
                                                    start=k == 0 and o == 0, stop=k == KC - 1, skip_group_check=True)
                    last.then_inc(block_used, 1)
                    if n % GROUP == GROUP - 1:
                        gates(mix, li, n // GROUP, loaded)
                pe.wait_ge(gates_free, 2 * KC * (li + 1))
                for j in range(OUT_BLOCKS):
                    b = mix["out"] + j
                    loaded(b)
                    pe.wait_ge(prod_ready, mix["prod"] + 2 * j + 2)
                    for t in range(TT):
                        for h in range(2):
                            for kk in range(2):
                                c0 = kk * D_MODEL + h * HALF
                                last = nc.tensor.matmul(down[:, t, h, :], feat_b[:, 2 * j + kk, t * P:(t + 1) * P],
                                                        raw[:, b % SLOTS, c0:c0 + HALF],
                                                        start=j == 0 and kk == 0, stop=j == OUT_BLOCKS - 1 and kk == 1)
                            if j == OUT_BLOCKS - 1 and (t, h) != (TT - 1, 1):
                                last.then_inc(down_done, 1)
                    last.then_inc(block_used, 1)

            def gates(mix, li, group, loaded):
                b = lru_gates(mix, group)
                loaded(b)
                for m in range(2 * GROUP):
                    n, d = GROUP * group + m // 2, m % 2
                    pair = 2 * n + d
                    if d == 0:
                        pe.wait_ge(up_free, mix["q"] + n + 1)
                    wait(pe, gates_free, 2 * KC * li + pair - 3 if pair > 3 else 0)
                    for o in range(2):
                        c0 = (2 * m + o) * P
                        last = nc.tensor.matmul(down[:, (pair % 4) // 2, pair % 2, o * SEQ:(o + 1) * SEQ],
                                                raw[:, b % SLOTS, c0:c0 + P], feat_b[:, n, :],
                                                start=o == 0, stop=True, skip_group_check=True)
                    last.then_inc(gates_done if m < 2 * GROUP - 1 else block_used, 1)

            def attention(mix):
                def scores(h):
                    p0, n = HEAD_DIM * (h % 2), h // 2
                    if h == 0:
                        pe.wait_ge(up_free, mix["q"] + mix["up"])
                    wait(pe, score_ready, TT * (h - 1))
                    for t in range(TT):
                        last = nc.tensor.matmul(up[:, h % 2, t * SEQ:(t + 1) * SEQ],
                                                feat_a[p0:p0 + HEAD_DIM, n, t * P:(t + 1) * P],
                                                feat_b[p0:p0 + HEAD_DIM, n, :],
                                                start=True, stop=True)
                    last.then_inc(scores_done, 1)

                def transpose_probs(h):
                    pe.wait_ge(probs_ready, TT * (h + 1))
                    wait(pe, pt_ready, h - 1)
                    for t in range(TT):
                        for kt in range(TT):
                            last = nc.tensor.transpose(
                                up[:, 2 + h % 2, kt * SEQ + t * P:kt * SEQ + (t + 1) * P],
                                probs[:, h % 4, t, kt * P:(kt + 1) * P], ident[:, :])
                    last.then_inc(pt_done, 1)

                def mix_values(h):
                    p0, n = HEAD_DIM * (h % 2), h // 2
                    pe.wait_ge(pt_ready, h + 1)
                    if n >= 4 and h % 2 == 0:
                        pe.wait_ge(act_lo_ready, mix["act"] + n - 3)
                    for kt in range(TT):
                        last = nc.tensor.matmul(down[p0:p0 + HEAD_DIM, (n % 4) // 2, n % 2, 0:SEQ],
                                                values[:, kt, h * HEAD_DIM:(h + 1) * HEAD_DIM],
                                                probs_t[:, h % 4, kt, :],
                                                start=kt == 0, stop=kt == TT - 1)
                    last.then_inc(pv_done, 1)

                pe.wait_ge(v_ready, 4)
                for h in range(HEADS + 3):
                    if h < HEADS:
                        scores(h)
                    if 2 <= h <= HEADS + 1:
                        transpose_probs(h - 2)
                    if h >= 3:
                        mix_values(h - 3)
                pe.wait_ge(act_lo_ready, mix["act"] + KC)

            pe.wait_ge(ident_ready, 2)
            pe.wait_ge(consts_ready, 2)
            li = 0
            for i, (kind, mix, ffn) in enumerate(LAYERS):
                if i == 0:
                    pe.wait_ge(c_ready, 1)
                    first_modulation(range(ADA_COLS // P))
                    transposes(0)
                    first_modulation((3, 4, 5, 6, 7, 8, 9, 10, 11, 14, 15, 12, 13)).then_inc(mod_t_done, 1)
                else:
                    transposes(2 * i)
                if kind == LRU:
                    lru(2 * i, mix, li)
                    li += 1
                    lrus[0] += 1
                else:
                    up_phase(mix["split_norms"], mix["b"], mix["up"], up_free, mix["q"])
                if kind == ATTENTION:
                    down_phase((h_hi, h_lo), mix["b"] + mix["up"], mix["mid"], 0, v_done, None)
                    attention(mix)
                if kind != LRU:
                    down_phase((act_hi, act_lo), mix["out"], OUT_BLOCKS, mix["act"], down_done, act_lo_ready)
                transposes(2 * i + 1)
                up_phase(ffn["split_norms"], ffn["b"], ffn["up"], prod_ready, ffn["prod"])
                down_phase((act_hi, act_lo), ffn["out"], FFN_DOWN, ffn["act"], down_done, act_lo_ready)

        @block.scalar
        def _(act):
            def round_block(b, s, r):
                if isinstance(b, int) and (b >= BLOCKS or plain(b)):
                    return
                act.wait_ge(raw_in[s], r * 16 + 16)
                wait(act, block_used, b - SLOTS + 1)
                nc.scalar.activation(w_hi[:, s, :], raw[:, s, :], ACT.Copy).then_inc(hi_ready, 1)

            def squares_m(u):
                for n, t, h, cs in quarters():
                    if n < 3:
                        act.wait_ge(down_done, 3 * u + n + 1)
                    else:
                        act.wait_ge(block_used, LAYERS[u // 2][1 + u % 2]["end"])
                    nc.scalar.activation(junk[:, n, :], down[:, t, h, :], ACT.Square, scale=ROOT_MEAN,
                                         accum_out=sq_m[:, n:n + 1]).then_inc(sq_m_ready, 1)

            def normed_x(v):
                for n, t, h, cs in quarters():
                    if v == 0:
                        act.wait_ge(x_loaded, 16 * TT)
                    else:
                        act.wait_ge(x_ready, 4 * (v - 1) + n + 1)
                    nc.scalar.activation(junk[:, n, :], x[:, t, cs], ACT.Square, scale=ROOT_MEAN,
                                         accum_out=sq_x[:, n:n + 1]).then_inc(sq_x_ready, 1)
                act.wait_ge(rs_x_ready, TT * (v + 1))
                nc.scalar.activation(tok[:, TT - 1, HALF:], x[:, TT - 1, HALF:], ACT.Copy,
                                     scale=rs_x[:, TT - 1:TT]).then_inc(xn_act_ready, 1)

            def modulated(v):
                src = norm_bank(v)
                act.wait_ge(mod_col_ready, v + 1)
                for k in range(KC):
                    act.wait_ge(xt_done, KC * v + (k | 1) + 1)
                    dst = h_plain if v % 2 == 0 and LAYERS[v // 2][0] == LRU else feat_b
                    nc.scalar.activation(dst[:, k, :], src[k], ACT.Identity,
                                         scale=scale_col[:, k:k + 1], bias=mod_col[:, k:k + 1])\
                        .then_inc(h_ready, 1)

            def ffn_up(ffn):
                def body(b, s, r):
                    j = b - ffn["b"]
                    act.wait_ge(block_used, b + 1)
                    nc.scalar.activation(side[:, s, :], up[:, s, 0:SEQ], ACT.Silu).then_inc(side_ready, 1)
                    round_block(b + SLOTS, s, r + 1)
                    act.wait_ge(prod_ready, j + ffn["prod"] + 1)
                    nc.scalar.activation(act_hi[:, j, :], prod[:, s, :], ACT.Copy).then_inc(act_hi_ready, 1)
                each_block(act, ffn["b"], ffn["up"], body)

            def down_rounds(first, n):
                while n > 0 and (first + n - 1 + SLOTS >= BLOCKS or plain(first + n - 1 + SLOTS)):
                    n -= 1
                each_block(act, first, n, lambda b, s, r: round_block(b + SLOTS, s, r + 1))

            def lru(mix, li):
                c0 = COL_LRU + li * LRU_COLS

                def conv(n):
                    b = lru_block(mix, n)
                    s = b % SLOTS
                    act.wait_ge(block_used, b + 1)
                    nc.scalar.activation(feat_c[:, n, :], up[:, s, 0:SEQ], ACT.Gelu_apprx_tanh)
                    nc.scalar.activation(feat_b[:, n, :], up[:, s, SEQ:2 * SEQ], ACT.Identity,
                                         scale=col[:, c0 + 2 * KC + n:c0 + 2 * KC + n + 1],
                                         bias=col[:, c0 + 4 * KC + n:c0 + 4 * KC + n + 1])\
                        .then_inc(conv_ready, 1)
                    round_block(b + SLOTS, s, b // SLOTS + 1)

                def sigmoids(g):
                    b = lru_gates(mix, g)
                    for m in range(2 * GROUP):
                        if m < 2 * GROUP - 1:
                            act.wait_ge(gates_done, (2 * li + g) * (2 * GROUP - 1) + m + 1)
                        else:
                            act.wait_ge(block_used, b + 1)
                        n, d = GROUP * g + m // 2, m % 2
                        bank = down[:, (m % 4) // 2, m % 2, :]
                        for o, dst in ((0, lru_r[g]), (1, lru_i[g])):
                            cb = c0 + (5 + 2 * d + o) * KC + n
                            last = nc.scalar.activation(dst[:, d, m // 2, :], bank[:, o * SEQ:(o + 1) * SEQ],
                                                        ACT.Sigmoid, bias=col[:, cb:cb + 1])
                        last.then_inc(gates_free, 1)
                    round_block(b + SLOTS, b % SLOTS, b // SLOTS + 1)

                def decays(g):
                    act.wait_ge(y_ready, 2 * KC * li + 2 * GROUP * (g + 1))
                    if g == 1:
                        act.wait_ge(w_ready, 4 * li + 2)
                        act.wait_ge(scans_done, 2 * li + 1)
                    for d in range(2):
                        y = lru_r[g][:, d, :, :]
                        nc.scalar.activation(lru_sq[:, d, :, :], y, ACT.Exp, scale=-2.0).then_inc(decay_ready, 1)
                        nc.scalar.activation(lru_a[g][:, d, :, :], y, ACT.Exp, scale=-1.0).then_inc(decay_ready, 1)
                        act.wait_ge(decay_ready, 12 * li + 6 * g + 3 * d + 2)
                        nc.scalar.activation(y, y, ACT.Tanh).then_inc(decay_ready, 1)

                def roots(g):
                    for d in range(2):
                        act.wait_ge(w_ready, 4 * li + 2 * g + d + 1)
                        nc.scalar.activation(lru_r[g][:, d, :, :], lru_r[g][:, d, :, :], ACT.Sqrt)\
                            .then_inc(root_ready, 1)

                for n in range(GROUP):
                    conv(n)
                sigmoids(0)
                decays(0)
                conv(GROUP)
                roots(0)
                for n in range(GROUP + 1, KC):
                    conv(n)
                sigmoids(1)
                decays(1)
                roots(1)
                act.wait_ge(acc_ready, 1 + EARLY)

            def by_row(v):
                return v.rearrange("p (r c) -> p r c", c=GRID_W)

            def attention(mix):
                def load_band(half, rl):
                    row = half * HEADS // 2 * RPB_ROWS + 5 - rl
                    off = row * RPB_COLS + RPB_COLS // 2 - (GRID_W - 1)
                    src = bass.AP(rpb.tensor, off, [[1, GRID_W], [RPB_ROWS * RPB_COLS, HEADS // 2], [1, BAND_RUN]])
                    act.dma_start(band_runs[half][rl * GRID_W:(rl + 1) * GRID_W, :, :], src).then_inc(band_in[half], 16)

                def spread_band(half):
                    act.wait_ge(band_in[half], 16 * 2)
                    run = band_runs[half][:, :, :]
                    src = bass.AP(run.tensor, run.offset,
                                  [run.ap[0], [BAND_RUN, HEADS // 2], [RPB_COLS, BAND], [1, GRID_W]])
                    nc.scalar.activation(bands[half][:, :, :, :], src, ACT.Copy).then_inc(band_spread, 1)

                def body(b, s, r):
                    n = b - mix["b"]
                    act.wait_ge(block_used, b + 1)
                    nc.scalar.activation(by_row(feat_a[:, n, :])[:, :, ::-1], by_row(up[:, s, 0:SEQ]), ACT.Copy,
                                         scale=HEAD_DIM ** -0.5).then_inc(q_ready, 1)
                    round_block(b + SLOTS, s, r + 1)
                    if n < 4:
                        load_band(n // 2, n % 2)
                    elif n < 6:
                        spread_band(n - 4)
                straight(act, mix["b"], mix["up"], body)
                down_rounds(mix["b"] + mix["up"], mix["mid"])
                for n in range(4):
                    if n < 3:
                        act.wait_ge(v_done, n + 1)
                    else:
                        act.wait_ge(block_used, mix["out"])
                    nc.scalar.activation(values[:, n // 2, (n % 2) * HALF:(n % 2 + 1) * HALF],
                                         down[:, n // 2, n % 2, :], ACT.Copy).then_inc(v_ready, 1)
                for h in range(HEADS + 4):
                    if h < HEADS:
                        act.wait_ge(neg_ready, h + 1)
                        for t in range(TT):
                            nc.scalar.activation(probs[:, h % 4, t, :], probs[:, h % 4, t, :], ACT.Exp,
                                                 bias=sneg[:, h % 4, t:t + 1],
                                                 accum_out=ssum[:, h % 4, t:t + 1]).then_inc(exp_ready, 1)
                    if 2 <= h <= HEADS + 1:
                        g = h - 2
                        act.wait_ge(pt_done, g + 1)
                        wait(act, pv_done, g - 3)
                        nc.scalar.activation(by_row(probs_t[:, g % 4, :, :].rearrange("p t s -> p (t s)")),
                                             by_row(up[:, 2 + g % 2, :])[:, :, ::-1], ACT.Copy)\
                            .then_inc(pt_ready, 1)
                    if h >= 5 and h % 2 == 1:
                        n = (h - 5) // 2
                        act.wait_ge(pv_done, 2 * n + 2)
                        if n == 0:
                            act.wait_ge(band_spread, 2)
                        nc.scalar.activation(act_hi[:, n, :], down[:, (n % 4) // 2, n % 2, 0:SEQ],
                                             ACT.Copy).then_inc(act_hi_ready, 1)

            def short_conv(mix):
                def pair(b, s, r):
                    n = b - mix["b"]
                    act.wait_ge(block_used, b + 1)
                    nc.scalar.activation(side[:, s, :], up[:, s, SEQ:2 * SEQ], ACT.Copy).then_inc(side_ready, 1)
                    round_block(b + SLOTS, s, r + 1)
                    act.wait_ge(up_free, mix["q"] + n + 1)
                    nc.scalar.activation(feat_c[:, n, :], feat_b[:, n, :], ACT.Copy,
                                         scale=col[:, COL_SC + KC + n:COL_SC + KC + n + 1]).then_inc(conv_ready, 1)
                straight(act, mix["b"], KC, pair)

                def gate(b, s, r):
                    j = b - mix["b"] - KC
                    round_block(b + SLOTS, s, r + 1)
                    act.wait_ge(up_free, mix["q"] + KC + j + 1)
                    for n in (2 * j, 2 * j + 1):
                        nc.scalar.activation(act_hi[:, n, :], feat_a[:, n, :], ACT.Copy).then_inc(act_hi_ready, 1)
                straight(act, mix["b"] + KC, mix["up"] - KC, gate)

            act.wait_ge(cols_in, 16)
            nc.scalar.activation(c_act[:, :], col[:, COL_C:COL_C + KC], ACT.Silu).then_inc(c_ready, 1)
            act.wait_ge(soft_step, 1)
            nc.scalar.activation(soft[:, 1, :], soft[:, 0, :], ACT.Exp, scale=-1.0).then_inc(soft_exp, 1)
            normed_x(0)
            modulated(0)
            li = 0
            for i, (kind, mix, ffn) in enumerate(LAYERS):
                if kind == LRU:
                    lru(mix, li)
                    li += 1
                elif kind == ATTENTION:
                    attention(mix)
                else:
                    short_conv(mix)
                late = 2 if kind == LRU else 1
                down_rounds(mix["out"], OUT_BLOCKS - late)
                squares_m(2 * i)
                normed_x(2 * i + 1)
                modulated(2 * i + 1)
                down_rounds(mix["end"] - late, late)
                ffn_up(ffn)
                down_rounds(ffn["out"], FFN_DOWN - 1)
                squares_m(2 * i + 1)
                if i < DEPTH - 1:
                    normed_x(2 * i + 2)
                    modulated(2 * i + 2)
                    down_rounds(ffn["end"] - 1, 1)

        @block.vector
        def _(dve):
            steps = [0, 0]

            def link(last, which=0):
                s = (soft_step, vector_step)[which]
                steps[which] += 1
                last.then_inc(s, 1)
                dve.wait_ge(s, steps[which])

            lrus = [0]

            def lo_block(b, s):
                if isinstance(b, int) and (b >= BLOCKS or plain(b)):
                    return
                dve.wait_ge(hi_ready, splits(b, lrus[0]))
                nc.vector.tensor_tensor(w_lo[:, s, :], raw[:, s, :], w_hi[:, s, :].bitcast(f32),
                                        ALU.subtract).then_inc(lo_ready, 1)

            def ada_block(a):
                src = ada_raw
                if isinstance(a, int) and a == ADA_HEAD:
                    dve.wait_ge(ada_in, 16)
                elif isinstance(a, int) and a <= ADA_HEAD + EARLY:
                    turn, i = divmod(a - ADA_HEAD - 1, EARLY_SLOTS)
                    dve.wait_ge(ada_early_in[i], 16 * (turn + 1))
                    src = ada_early[i]
                else:
                    dve.wait_ge(ada_in, a * 16 + 16 * (1 - ADA_HEAD - EARLY))
                wait(dve, acc_free, a - ADA_HEAD)
                nc.vector.tensor_scalar(ada_acc[:, :], src[:, 0, :], c_act[:, 0:1], None, ALU.mult)\
                    .then_inc(acc_step, 1)
                for k in range(1, KC):
                    dve.wait_ge(acc_step, a * (KC - 1) + (k - ADA_HEAD * (KC - 1)))
                    last = nc.vector.scalar_tensor_tensor(ada_acc[:, :], src[:, k, :], c_act[:, k:k + 1],
                                                          ada_acc[:, :], ALU.mult, ALU.add)
                    last.then_inc(acc_step if k < KC - 1 else acc_ready, 1)

            def ada_behind(b):
                a = ada_after(b)
                if a is not None:
                    ada_block(a)

            def prepare(b, s, r):
                lo_block(b + SLOTS, s)
                if isinstance(b, int):
                    ada_behind(b)
                elif s == SLOTS - 1 and ada_in_loop[0]:
                    ada_block(r + 11)

            ada_in_loop = [True]

            def post_norm(u):
                dve.wait_ge(gate_row_ready, u + 1)
                for tile in range(TT):
                    for n, t, h, cs in quarters():
                        if t == tile:
                            dve.wait_ge(sq_m_ready, 4 * u + n + 1)
                            nc.vector.tensor_tensor(tok[:, t, cs], down[:, t, h, :], gate_row[:, cs], ALU.mult)\
                                .then_inc(delta_ready, 1)
                    dve.wait_ge(rs_m_ready, TT * u + tile + 1)
                    for n, t, h, cs in quarters():
                        if t == tile:
                            dve.wait_ge(delta_ready, 4 * u + n + 1)
                            nc.vector.scalar_tensor_tensor(x[:, t, cs], tok[:, t, cs], rs_m[:, t:t + 1], x[:, t, cs],
                                                           ALU.mult, ALU.add).then_inc(x_ready, 1)

            def modulation(v):
                i, part = divmod(v, 2)
                dve.wait_ge(mod_t_done, v + 1)
                cb = COL_ADA_B + (6 * i + 3 * part) * KC
                nc.vector.tensor_tensor(mod_col[:, :], up[:, first_slot(v), 0:2 * KC],
                                        col[:, cb:cb + 2 * KC], ALU.add).then_inc(mod_col_step, 1)
                dve.wait_ge(mod_col_step, v + 1)
                cn = COL_NORM + v * KC
                nc.vector.scalar_tensor_tensor(scale_col[:, :], mod_col[:, KC:2 * KC], 1.0, col[:, cn:cn + KC],
                                               ALU.add, ALU.mult).then_inc(mod_col_ready, 1)

            def normed_x(v):
                for t in range(TT):
                    dve.wait_ge(rs_x_ready, TT * v + t + 1)
                    cs = slice(0, D_MODEL if t < TT - 1 else HALF)
                    nc.vector.tensor_scalar(tok[:, t, cs], x[:, t, cs], rs_x[:, t:t + 1], None, ALU.mult)\
                        .then_inc(xn_ready, 1)

            def split_h(v):
                if v % 2 == 0 and LAYERS[v // 2][0] == LRU:
                    return
                norms = LAYERS[v // 2][1 + v % 2]["split_norms"]
                for k in range(KC):
                    dve.wait_ge(h_ready, KC * v + k + 1)
                    nc.vector.tensor_copy(h_hi[:, k, :], feat_b[:, k, :]).then_inc(h_hi_ready, 1)
                    if k % 2 == 0:
                        dve.wait_ge(h_hi_ready, KC * norms + k + 1)
                        nc.vector.tensor_tensor(h_lo[:, k, :], feat_b[:, k, :], h_hi[:, k, :].bitcast(f32),
                                                ALU.subtract).then_inc(h_lo_even, 1)

            def boundary(u, end):
                post_norm(u)
                if u + 1 < 2 * DEPTH:
                    normed_x(u + 1)
                    modulation(u + 1)
                    split_h(u + 1)
                for b in (end - 2, end - 1):
                    lo_block(b + SLOTS, b % SLOTS)
                for b in (end - 2, end - 1):
                    ada_behind(b)

            def ffn_up(ffn):
                def body(b, s, r):
                    j = b - ffn["b"]
                    dve.wait_ge(side_ready, j + ffn["side"] + 1)
                    if not isinstance(j, int) or j >= SLOTS:
                        dve.wait_ge(act_lo_ready, j + (ffn["act"] - SLOTS + 1))
                    nc.vector.tensor_tensor(prod[:, s, :], side[:, s, :], up[:, s, SEQ:2 * SEQ], ALU.mult)\
                        .then_inc(prod_ready, 1)
                    prepare(b, s, r)
                straight(dve, ffn["b"], SLOTS, body)
                each_block(dve, ffn["b"] + SLOTS, ffn["up"] - SLOTS, body)

            def lru(mix, li):
                c0 = COL_LRU + li * LRU_COLS

                def tap(k, n):
                    return col[:, c0 + k * KC + n:c0 + k * KC + n + 1]

                def conv(n):
                    b = lru_block(mix, n)
                    s = b % SLOTS
                    src = up[:, s, SEQ:2 * SEQ]
                    dve.wait_ge(conv_ready, mix["conv"] + n + 1)
                    for m, (k, d) in enumerate(((0, 2), (1, 1), (3, -1))):
                        lo, hi = max(d, 0), SEQ + min(d, 0)
                        if m:
                            dve.wait_ge(conv_step, 2 * (KC * li + n) + m)
                        last = nc.vector.scalar_tensor_tensor(
                            feat_b[:, n, lo:hi], src[:, lo - d:hi - d], tap(k, n), feat_b[:, n, lo:hi],
                            ALU.mult, ALU.add)
                        last.then_inc(conv_step if m < 2 else up_free, 1)

                def decay_exponents(g):
                    for m in range(2 * GROUP):
                        n, d = GROUP * g + m // 2, m % 2
                        dve.wait_ge(gates_free, 2 * KC * li + 2 * n + d + 1)
                        cs = (li * 2 + d) * KC + n
                        nc.vector.tensor_scalar(lru_r[g][:, d, m // 2, :], lru_r[g][:, d, m // 2, :],
                                                soft[:, 5, cs:cs + 1], None, ALU.mult).then_inc(y_ready, 1)

                def weights(g):
                    for d in range(2):
                        dve.wait_ge(decay_ready, 12 * li + 6 * g + 3 * d + 3)
                        nc.vector.scalar_tensor_tensor(lru_r[g][:, d, :, :], lru_sq[:, d, :, :], 1.0,
                                                       lru_r[g][:, d, :, :], ALU.add, ALU.mult).then_inc(w_ready, 1)

                def scans(g):
                    for d in range(2):
                        dve.wait_ge(root_ready, 4 * li + 2 * g + d + 1)
                        dve.wait_ge(ix_ready, 2 * KC * li + 2 * GROUP * (g + 1))
                        link(nc.vector.tensor_tensor(lru_r[g][:, d, :, :], lru_r[g][:, d, :, :],
                                                     lru_i[g][:, d, :, :], ALU.mult), 1)
                        step = 1 if d == 0 else -1
                        for m in range(GROUP):
                            last = nc.vector.tensor_tensor_scan(lru_i[g][:, d, m, ::step], lru_a[g][:, d, m, ::step],
                                                                lru_r[g][:, d, m, ::step], 0.0, ALU.mult, ALU.add)
                    last.then_inc(scans_done, 1)

                def mixed(g):
                    dve.wait_ge(scans_done, 2 * li + g + 1)
                    link(nc.vector.tensor_tensor(lru_i[g][:, 0, :, :], lru_i[g][:, 0, :, :], lru_i[g][:, 1, :, :],
                                                 ALU.add), 1)
                    for m in range(GROUP):
                        n = GROUP * g + m
                        nc.vector.tensor_tensor(feat_b[:, n, :], lru_i[g][:, 0, m, :], feat_c[:, n, :], ALU.mult)\
                            .then_inc(prod_ready, 1)

                for n in range(GROUP):
                    conv(n)
                    if n > 0:
                        ada_behind(lru_block(mix, n - 1))
                decay_exponents(0)
                ada_behind(lru_block(mix, GROUP - 1))
                weights(0)
                conv(GROUP)
                ada_behind(lru_gates(mix, 0))
                for n in range(GROUP + 1, KC - 1):
                    conv(n)
                    ada_behind(lru_block(mix, n - 1))
                if li > 0:
                    scans(0)
                    mixed(0)
                conv(KC - 1)
                if li == 0:
                    scans(0)
                    mixed(0)
                decay_exponents(1)
                ada_behind(lru_block(mix, KC - 2))
                weights(1)
                scans(1)
                mixed(1)
                ada_behind(lru_block(mix, KC - 1))
                ada_behind(lru_gates(mix, 1))

            def attention(mix):
                def body(b, s, r):
                    n = b - mix["b"]
                    dve.wait_ge(q_ready, n + 1)
                    nc.vector.tensor_copy(feat_b[:, n, :], up[:, s, SEQ:2 * SEQ]).then_inc(up_free, 1)
                    prepare(b, s, r)
                straight(dve, mix["b"], mix["up"], body)
                straight(dve, mix["b"] + mix["up"], mix["mid"], prepare)
                for h in range(HEADS + 4):
                    if h < HEADS:
                        dve.wait_ge(scores_done, h + 1)
                        if h % 8 == 0:
                            dve.wait_ge(band_ready, 4 * (h // 8 + 1))
                        wait(dve, pt_done, h - 3)
                        band = bands[h // 8][:, h % 8, :, :].rearrange("p j c -> p (j c)")
                        for t in range(TT):
                            j0 = (2 - 2 * t) * GRID_W
                            nc.vector.tensor_tensor_reduce(
                                out=probs[:, h % 4, t, :], in0=up[:, h % 2, t * SEQ:(t + 1) * SEQ],
                                in1=band[:, j0:j0 + SEQ], scale=1.0, scalar=-3e38, op0=ALU.add, op1=ALU.max,
                                accum_out=smax[:, h % 4, t:t + 1]).then_inc(score_ready, 1)
                        dve.wait_ge(score_ready, TT * (h + 1))
                        nc.vector.tensor_scalar(sneg[:, h % 4, :], smax[:, h % 4, :], -1.0, None, ALU.mult)\
                            .then_inc(neg_ready, 1)
                    if 1 <= h <= HEADS:
                        g = h - 1
                        dve.wait_ge(exp_ready, TT * (g + 1))
                        nc.vector.reciprocal(sinv[:, g % 4, :], ssum[:, g % 4, :]).then_inc(inv_ready, 1)
                        dve.wait_ge(inv_ready, g + 1)
                        for t in range(TT):
                            nc.vector.tensor_scalar(probs[:, g % 4, t, :], probs[:, g % 4, t, :],
                                                    sinv[:, g % 4, t:t + 1], None, ALU.mult)\
                                .then_inc(probs_ready, 1)
                    if h >= 5 and h % 2 == 1:
                        n = (h - 5) // 2
                        dve.wait_ge(act_hi_ready, mix["act"] + n + 1)
                        nc.vector.tensor_tensor(act_lo[:, n, :], down[:, (n % 4) // 2, n % 2, 0:SEQ],
                                                act_hi[:, n, :].bitcast(f32), ALU.subtract).then_inc(act_lo_ready, 1)

            def short_conv(mix):
                def pair(b, s, r):
                    n = b - mix["b"]
                    dve.wait_ge(side_ready, mix["side"] + n + 1)
                    nc.vector.tensor_tensor(feat_b[:, n, :], up[:, s, 0:SEQ], side[:, s, :], ALU.mult)\
                        .then_inc(up_free, 1)
                    prepare(b, s, r)
                    dve.wait_ge(conv_ready, mix["conv"] + n + 1)
                    for k, d in ((0, 1), (2, -1)):
                        lo, hi = max(d, 0), SEQ + min(d, 0)
                        w = col[:, COL_SC + k * KC + n:COL_SC + k * KC + n + 1]
                        link(nc.vector.scalar_tensor_tensor(
                            feat_c[:, n, lo:hi], feat_b[:, n, lo - d:hi - d], w, feat_c[:, n, lo:hi],
                            ALU.mult, ALU.add), 1)
                straight(dve, mix["b"], KC, pair)

                def gate(b, s, r):
                    j = b - mix["b"] - KC
                    dve.wait_ge(block_used, b + 1)
                    two = slice(2 * j * SEQ, (2 * j + 2) * SEQ)
                    nc.vector.tensor_tensor(buf_a[:, two], up[:, s, :], buf_c[:, two], ALU.mult)\
                        .then_inc(up_free, 1)
                    prepare(b, s, r)
                straight(dve, mix["b"] + KC, mix["up"] - KC, gate)

            dve.wait_ge(cols_in, 16)
            lam = [soft[:, n, :] for n in range(6)]
            for li in range(N_LRU):
                c0 = COL_LRU + li * LRU_COLS + 9 * KC
                lam_col = col[:, c0:c0 + 2 * KC]
                last = nc.vector.scalar_tensor_tensor(lam[0][:, li * 2 * KC:(li + 1) * 2 * KC], lam_col, -1.0,
                                                      lam_col, ALU.mult, ALU.max)
            link(last)
            normed_x(0)
            for li in range(N_LRU):
                c0 = COL_LRU + li * LRU_COLS + 9 * KC
                last = nc.vector.tensor_scalar(lam[5][:, li * 2 * KC:(li + 1) * 2 * KC], col[:, c0:c0 + 2 * KC],
                                               -1.0, 0.0, ALU.mult, ALU.max)
            link(last)
            dve.wait_ge(soft_exp, 1)
            link(nc.vector.tensor_scalar(lam[2], lam[1], 2.0, None, ALU.add))
            link(nc.vector.reciprocal(lam[3], lam[2]))
            link(nc.vector.tensor_tensor(lam[2], lam[1], lam[3], ALU.mult))
            link(nc.vector.tensor_tensor(lam[3], lam[2], lam[2], ALU.mult))
            terms = 9
            link(nc.vector.tensor_scalar(lam[4], lam[3], 2.0 / (2 * terms + 1), 2.0 / (2 * terms - 1), ALU.mult, ALU.add))
            for n in range(terms - 2, -1, -1):
                link(nc.vector.tensor_tensor(lam[4], lam[4], lam[3], ALU.mult))
                link(nc.vector.tensor_scalar(lam[4], lam[4], 2.0 / (2 * n + 1), None, ALU.add))
            link(nc.vector.tensor_tensor(lam[4], lam[4], lam[2], ALU.mult))
            link(nc.vector.tensor_tensor(lam[5], lam[5], lam[4], ALU.add))
            link(nc.vector.tensor_scalar(lam[5], lam[5], LRU_C, None, ALU.mult))

            dve.wait_ge(c_ready, 1)
            for a in range(1, ADA_HEAD):
                dve.wait_ge(ada_head_in[a], 16)
                width = P * sum(j not in HEAD_ALONE for j in range(ADA_COLS // P * a, ADA_COLS // P * (a + 1)))
                acc = ada_head[a][:, 0, 0:width]
                nc.vector.tensor_scalar(acc, acc, c_act[:, 0:1], None, ALU.mult).then_inc(head_step, 1)
                for k in range(1, KC):
                    dve.wait_ge(head_step, (a - 1) * (KC - 1) + k)
                    last = nc.vector.scalar_tensor_tensor(acc, ada_head[a][:, k, 0:width], c_act[:, k:k + 1], acc,
                                                          ALU.mult, ALU.add)
                    last.then_inc(head_step if k < KC - 1 else head_ready, 1)
            modulation(0)
            ada_block(ADA_HEAD)
            li = 0
            for i, (kind, mix, ffn) in enumerate(LAYERS):
                if kind == LRU:
                    lru(mix, li)
                    li += 1
                    lrus[0] += 1
                elif kind == ATTENTION:
                    attention(mix)
                else:
                    short_conv(mix)
                straight(dve, mix["out"], OUT_BLOCKS - 2, prepare)
                boundary(2 * i, mix["end"])
                ada_in_loop[0] = ada_after(ffn["end"] - 1 - (ffn["end"] % SLOTS)) is not None
                ffn_up(ffn)
                each_block(dve, ffn["out"], FFN_DOWN - SLOTS, prepare)
                straight(dve, ffn["end"] - SLOTS, SLOTS - 2, prepare)
                boundary(2 * i + 1, ffn["end"])

        @block.gpsimd
        def _(pool):
            def inverse_rms(sums, arrived, count, t, dst, ready):
                pool.wait_ge(arrived, count - 1)
                nc.gpsimd.tensor_scalar(part[:, t:t + 1], sums[:, 2 * t:2 * t + 1], EPS, None, ALU.add)\
                    .then_inc(part_ready, 1)
                parts[0] += 1
                pool.wait_ge(part_ready, parts[0])
                pool.wait_ge(arrived, count)
                nc.gpsimd.tensor_tensor(part[:, t:t + 1], part[:, t:t + 1], sums[:, 2 * t + 1:2 * t + 2], ALU.add)\
                    .then_inc(part_ready, 1)
                parts[0] += 1
                pool.wait_ge(part_ready, parts[0])
                nc.gpsimd.tensor_tensor(dst[:, t:t + 1], part[:, t:t + 1], minus_half, ALU.pow).then_inc(ready, 1)

            parts = [0]

            def early(a):
                return isinstance(a, int) and ADA_HEAD < a <= ADA_HEAD + EARLY

            def rows_out(n):
                if n <= ADA_HEAD + EARLY + 1:
                    pool.wait_ge(mod_out, 16)
                    for i in range(2):
                        wait(pool, early_out[i], 16 * sum(early(a) and a % 2 == i for a in range(n)))
                else:
                    pool.wait_ge(mod_out, 16 * (n - ADA_HEAD - EARLY))

            def sum_ada(a):
                pool.wait_ge(acc_ready, a - (ADA_HEAD - 1))
                place, arrival = 0, mod_out
                if early(a):
                    place, arrival = a % 2, early_out[a % 2]
                    if a == ADA_HEAD + 1:
                        pool.wait_ge(mod_out, 16)
                    wait(pool, arrival, 16 * ((a - ADA_HEAD - 1) // 2))
                elif not isinstance(a, int) or a > ADA_HEAD:
                    pool.wait_ge(mod_out, a * 16 + 16 * -(ADA_HEAD + EARLY))
                pool.sem_inc(sum_turn, 1)
                nc.gpsimd.partition_all_reduce(ada_sum[:, place, :], ada_acc[:, :], P, bass.bass_isa.ReduceOp.add)\
                    .then_inc(acc_free, 1)
                pool.wait_ge(acc_free, a - (ADA_HEAD - 1))
                pool.dma_start(mod_rows[a], ada_sum[0:1, place, :]).then_inc(arrival, 16)

            def mod_at(i, group, rows):
                off = (6 * i + group) * D_MODEL
                return off, -(-(off + rows * P) // ADA_COLS)

            def load_mod_row(v):
                i, part = divmod(v, 2)
                off, n = mod_at(i, 3 * part, 2 * KC)
                rows_out(n)
                wait(pool, mod_t_done, v)
                pool.dma_start(mod_row[:, :], bass.AP(mod_dram, off, [[P, 2 * KC], [1, P]]))\
                    .then_inc(mod_row_in, 16)

            def load_gate_row(u):
                i, part = divmod(u, 2)
                group = 3 * part + 2
                off, n = mod_at(i, group, KC)
                rows_out(n)
                wait(pool, x_ready, 4 * u)
                every = [[0, P], [1, D_MODEL]]
                pool.dma_start(gate_row[:, :], bass.AP(mod_dram, off, every)).then_inc(rows_in, 16)
                pool.dma_start(bias_row[:, :], bass.AP(ada_b.tensor, (6 * i + group) * D_MODEL, every))\
                    .then_inc(rows_in, 16)
                pool.dma_start(norm_row[:, :], bass.AP(norm_g.tensor, (4 * i + 2 * part + 1) * D_MODEL, every))\
                    .then_inc(rows_in, 16)

            def make_gate_row(u):
                pool.wait_ge(rows_in, 48 * (u + 1))
                nc.gpsimd.tensor_tensor(gate_row[:, :], gate_row[:, :], bias_row[:, :], ALU.add)\
                    .then_inc(gate_sum_ready, 1)
                pool.wait_ge(gate_sum_ready, u + 1)
                nc.gpsimd.tensor_tensor(gate_row[:, :], gate_row[:, :], norm_row[:, :], ALU.mult)\
                    .then_inc(gate_row_ready, 1)

            def behind(b, s, r):
                if isinstance(b, int):
                    if b in row_work:
                        step, u = row_work[b]
                        step(u)
                    if ada_after(b) is not None:
                        sum_ada(ada_after(b))
                elif s == SLOTS - 1 and ada_in_loop[0]:
                    sum_ada(r + 11)

            ada_in_loop = [True]
            row_work = {}
            for i, (kind, mix, ffn) in enumerate(LAYERS):
                row_work[mix["b"] + 3] = (load_gate_row, 2 * i)
                row_work[lru_block(mix, KC - 2) if kind == LRU else mix["b"] + 7] = (make_gate_row, 2 * i)

            def norms(u, v):
                if u is not None:
                    for t in range(TT):
                        inverse_rms(sq_m, sq_m_ready, 4 * u + 2 * t + 2, t, rs_m, rs_m_ready)
                if v is not None:
                    for t in range(TT):
                        inverse_rms(sq_x, sq_x_ready, 4 * v + 2 * t + 2, t, rs_x, rs_x_ready)
                    for k in range(1, KC, 2) if v % 2 or LAYERS[v // 2][0] != LRU else ():
                        pool.wait_ge(h_hi_ready, KC * LAYERS[v // 2][1 + v % 2]["split_norms"] + k + 1)
                        nc.gpsimd.tensor_tensor(h_lo[:, k, :], feat_b[:, k, :], h_hi[:, k, :].bitcast(f32),
                                                ALU.subtract).then_inc(h_lo_odd, 1)

            def act_low(n, src, base):
                pool.wait_ge(act_hi_ready, n + (base + 1))
                nc.gpsimd.tensor_tensor(act_lo[:, n, :], src, act_hi[:, n, :].bitcast(f32), ALU.subtract)\
                    .then_inc(act_lo_ready, 1)

            def out_phase(u, first, n):
                end = first + n
                if u + 1 < 2 * DEPTH:
                    load_mod_row(u + 1)
                if n > OUT_BLOCKS:
                    load_gate_row(u)
                    each_block(pool, first, n - OUT_BLOCKS, behind)
                    make_gate_row(u)
                straight(pool, end - OUT_BLOCKS, OUT_BLOCKS - 2, behind)
                norms(u, u + 1 if u + 1 < 2 * DEPTH else None)
                straight(pool, end - 2, 2, behind)

            def lru(mix, li):
                b0 = mix["b"]
                for g in range(2):
                    for b in range(b0, b0 + GROUP - 1) if g == 0 else range(lru_gates(mix, 0), lru_block(mix, KC - 2)):
                        behind(b, b % SLOTS, b // SLOTS)
                    for m in range(2 * GROUP):
                        n, d = GROUP * g + m // 2, m % 2
                        pool.wait_ge(gates_free, 2 * KC * li + 2 * n + d + 1)
                        nc.gpsimd.tensor_tensor(lru_i[g][:, d, m // 2, :], lru_i[g][:, d, m // 2, :],
                                                feat_b[:, n, :], ALU.mult).then_inc(ix_ready, 1)
                    for b in (lru_block(mix, GROUP - 1),) if g == 0 else range(lru_block(mix, KC - 2), mix["out"]):
                        behind(b, b % SLOTS, b // SLOTS)

            def attention(mix):
                def mask(half, rl):
                    pool.wait_ge(band_spread, half + 1)
                    part = bands[half][rl * GRID_W:(rl + 1) * GRID_W, :, :, :].rearrange("p h j c -> p (h j) c")
                    rows = HEADS // 2 * BAND
                    low, high = part[:, :, 0:48], part[:, :, 16:GRID_W]
                    nc.gpsimd.affine_select(out=low, in_=low, compare_op=ALU.is_ge, fill=NEG, base=8 - (GRID_W - 1),
                                            pattern=[[0, rows], [1, 48]], channel_multiplier=1)\
                        .then_inc(band_ready, 1)
                    pool.wait_ge(band_ready, 4 * half + 2 * rl + 1)
                    nc.gpsimd.affine_select(out=high, in_=high, compare_op=ALU.is_ge, fill=NEG, base=GRID_W - 1 + 7 - 16,
                                            pattern=[[0, rows], [-1, 48]], channel_multiplier=-1)\
                        .then_inc(band_ready, 1)
                    pool.wait_ge(band_ready, 4 * half + 2 * rl + 2)

                straight(pool, mix["b"], mix["up"], behind)
                for rl in range(2):
                    mask(0, rl)
                    straight(pool, mix["b"] + mix["up"] + rl, 1, behind)
                straight(pool, mix["b"] + mix["up"] + 2, mix["mid"] - 2, behind)
                for rl in range(2):
                    mask(1, rl)

            def short_conv(mix):
                straight(pool, mix["b"], KC, behind)

                def gate(b, s, r):
                    j = b - mix["b"] - KC
                    for n in (2 * j, 2 * j + 1):
                        act_low(n, feat_a[:, n, :], mix["act"])
                    behind(b, s, r)
                straight(pool, mix["b"] + KC, mix["up"] - KC, gate)

            def ffn_up(ffn):
                def body(b, s, r):
                    act_low(b - ffn["b"], prod[:, s, :], ffn["act"])
                    behind(b, s, r)
                each_block(pool, ffn["b"], ffn["up"], body)

            nc.gpsimd.memset(minus_half, -0.5).then_inc(consts_ready, 1)
            nc.gpsimd.memset(ones, 1.0).then_inc(consts_ready, 1)
            nc.gpsimd.memset(ident[:, :], 0.0).then_inc(ident_ready, 1)
            pool.wait_ge(ident_ready, 1)
            nc.gpsimd.affine_select(out=ident[:, :], in_=ident[:, :], compare_op=ALU.not_equal, fill=1.0,
                                    base=0, pattern=[[-1, P]], channel_multiplier=1).then_inc(ident_ready, 1)
            pool.wait_ge(consts_ready, 2)
            norms(None, 0)
            sum_ada(ADA_HEAD)
            li = 0
            for i, (kind, mix, ffn) in enumerate(LAYERS):
                if kind == LRU:
                    lru(mix, li)
                    li += 1
                elif kind == ATTENTION:
                    attention(mix)
                else:
                    short_conv(mix)
                out_phase(2 * i, mix["out"], OUT_BLOCKS)
                ada_in_loop[0] = ada_after(ffn["end"] - 1 - (ffn["end"] % SLOTS)) is not None
                ffn_up(ffn)
                out_phase(2 * i + 1, ffn["out"], FFN_DOWN)


def _counts():
    side = prod = conv = 0
    for kind, mix, ffn in LAYERS:
        mix.update(side=side, prod=prod, conv=conv)
        if kind == SHORT_CONV:
            side += KC
        if kind == LRU:
            prod += KC
        if kind != ATTENTION:
            conv += KC
        ffn.update(side=side, prod=prod)
        side += FC
        prod += FC


_counts()


def _up_blocks(wa, wb):
    n = wa.shape[1] // P
    both = np.stack([w.reshape(KC, P, n, P) for w in (wa, wb)])
    return both.transpose(3, 2, 1, 0, 4).reshape(n, P, BLOCK)


def _down_blocks(w):
    return w.reshape(-1, 2, P, D_MODEL).transpose(0, 2, 1, 3).reshape(-1, P, BLOCK)


def _columns(v):
    return np.ascontiguousarray(v.reshape(-1, P).T)


def kernel(x, c, ada_w, ada_b, norm_g, ffn_w_gu, ffn_w_down,
           lru_w_in, lru_conv_w, lru_conv_b, lru_gate_w, lru_gate_b, lru_lambda, lru_w_out,
           na_w_qkv, na_rpb, na_w_o, sc_w_in, sc_conv_w, sc_w_out):
    import concourse.bacc as bacc
    from concourse.bass_utils import run_bass_kernel_spmd

    D = D_MODEL
    blocks = []
    for i, kind in enumerate(KINDS):
        j = i // 3
        if kind == LRU:
            w = np.asarray(lru_w_in[j])
            ups = _up_blocks(w[:, :D], w[:, D:])
            gates = np.asarray(lru_gate_w[j]).reshape(2, 2, 2, GROUP, P, P).transpose(2, 4, 3, 0, 1, 5)
            gates = gates.reshape(2, 1, P, BLOCK)
            for g in range(2):
                blocks += [ups[GROUP * g:GROUP * (g + 1)], gates[g]]
            blocks.append(_down_blocks(np.asarray(lru_w_out[j])))
        elif kind == ATTENTION:
            w = np.asarray(na_w_qkv[j])
            blocks.append(_up_blocks(w[:, :D], w[:, D:2 * D]))
            blocks.append(_down_blocks(np.ascontiguousarray(w[:, 2 * D:])))
            blocks.append(_down_blocks(np.asarray(na_w_o[j])))
        else:
            w = np.asarray(sc_w_in[j])
            blocks.append(_up_blocks(w[:, D:2 * D], w[:, 2 * D:]))
            b_gate = w[:, :D].reshape(D, KC // 2, 2, P)
            blocks.append(_up_blocks(b_gate[:, :, 0].reshape(D, D // 2), b_gate[:, :, 1].reshape(D, D // 2)))
            blocks.append(_down_blocks(np.asarray(sc_w_out[j])))
        w = np.asarray(ffn_w_gu[i])
        blocks.append(_up_blocks(w[:, :FFN_HIDDEN], w[:, FFN_HIDDEN:]))
        blocks.append(_down_blocks(np.asarray(ffn_w_down[i])))
    stream = np.concatenate(blocks)
    ada = np.asarray(ada_w).reshape(DEPTH, KC, P, 6 * D // ADA_COLS, ADA_COLS)
    ada = np.ascontiguousarray(ada.transpose(0, 3, 2, 1, 4).reshape(ADA_BLOCKS, P, KC * ADA_COLS))
    norm = np.asarray(norm_g)
    parts = [_columns(np.asarray(c)), _columns(np.asarray(ada_b)),
             _columns(np.ascontiguousarray(norm[:, 0::2]))]
    for li in range(N_LRU):
        parts += [_columns(np.asarray(a[li])) for a in (lru_conv_w, lru_conv_b, lru_gate_b, lru_lambda)]
    parts.append(_columns(np.asarray(sc_conv_w)))
    arrays = {
        "stream": stream, "ada": ada, "cols": np.concatenate(parts, axis=1),
        "x_in": np.asarray(x).reshape(SEQ, D), "norm": norm.reshape(-1), "ada_bias": np.asarray(ada_b).reshape(-1),
        "rpb_flat": np.asarray(na_rpb).reshape(-1),
    }
    nc = bacc.Bacc("TRN2", target_bir_lowering=False, num_devices=1)
    args = []
    for name, a in arrays.items():
        arrays[name] = np.ascontiguousarray(a)
        args.append(nc.dram_tensor(name, a.shape, mybir.dt.from_np(a.dtype), kind="ExternalInput").ap())
    out = nc.dram_tensor("out", (SEQ, D), mybir.dt.float32, kind="ExternalOutput").ap()
    encoder(nc, *args, out)
    r = run_bass_kernel_spmd(nc, [arrays], core_ids=[0])
    return r.results[0]["out"].reshape(1, SEQ, D)
```
